# Optimizing a Trainium2 kernel written in Bass

```python
import math
import jax, jax.numpy as jnp
from jax import lax
import numpy as np

D_MODEL = 1024
BATCH = 1
SEQ = 256
DEPTH = 2

N_A_LAYERS = DEPTH // 2
N_B_LAYERS = DEPTH - N_A_LAYERS

RET_HEADS = 4
RET_QK_DIM = D_MODEL // RET_HEADS
RET_V_DIM = 2 * RET_QK_DIM
RET_CHUNK = 128
ROPE_BASE = 10000.0

DIL_WINDOWS = (128, 512, 2048)
DIL_RATES = (1, 4, 16)
N_GROUPS = 3
DIL_HEADS = 16
DIL_HEAD_DIM = D_MODEL // DIL_HEADS
SUB_BLOCK = 128

NUM_BUCKETS = 32
MAX_DISTANCE = 2048

MOE_GROUPS = 4
EXPERTS_PER_GROUP = 8
N_EXPERTS = MOE_GROUPS * EXPERTS_PER_GROUP
TOP_K_INNER = 2
EXPERT_FF = D_MODEL // 2
MOE_BLOCK = 256

EPS = 1e-6
NEG_INF = -1e30

kernel_name = "yoco_retention_dilated_hmoe"

def rmsnorm(x, g):
    xf = x.astype(jnp.float32)
    y = xf * lax.rsqrt(jnp.mean(xf * xf, axis=-1, keepdims=True) + EPS)
    return (y * g.astype(jnp.float32)).astype(x.dtype)

def head_rmsnorm(t, g):
    tf = t.astype(jnp.float32)
    y = tf * lax.rsqrt(jnp.mean(tf * tf, axis=-1, keepdims=True) + EPS)
    return (y * g.astype(jnp.float32)).astype(t.dtype)

def rotary(t, pos):
    half = t.shape[-1] // 2
    inv = 1.0 / (ROPE_BASE ** jnp.linspace(0.0, 1.0, half, dtype=jnp.float32))
    ang = pos[:, None] * inv[None, :]
    cos = jnp.cos(ang)[None, :, None, :]
    sin = jnp.sin(ang)[None, :, None, :]
    tf = t.astype(jnp.float32)
    t1, t2 = tf[..., :half], tf[..., half:]
    return jnp.concatenate([t1 * cos - t2 * sin, t1 * sin + t2 * cos], axis=-1).astype(t.dtype)

def retention(xn, w_in, w_out):
    B, S, D = xn.shape
    H, dk, dv, C = RET_HEADS, RET_QK_DIM, RET_V_DIM, RET_CHUNK
    nC = S // C
    proj = xn @ w_in
    q, k, v, gate = jnp.split(proj, [H * dk, 2 * H * dk, 2 * H * dk + H * dv], axis=-1)
    pos = jnp.arange(S, dtype=jnp.float32)
    q = rotary(q.reshape(B, S, H, dk), pos)
    k = rotary(k.reshape(B, S, H, dk), pos) * (dk ** -0.5)
    v = v.reshape(B, S, H, dv)

    log_g = jnp.log(1.0 - 2.0 ** (-5.0 - jnp.arange(H, dtype=jnp.float32)))
    idx = jnp.arange(C, dtype=jnp.float32)
    diff = idx[:, None] - idx[None, :]
    d_in = jnp.where(diff >= 0, jnp.exp(log_g[:, None, None] * jnp.maximum(diff, 0.0)), 0.0)
    xi = jnp.exp(log_g[:, None] * (idx + 1.0))
    zeta = jnp.exp(log_g[:, None] * (C - 1.0 - idx))
    chunk_decay = jnp.exp(log_g * C)

    def chunks(t):
        return t.reshape(B, nC, C, H, -1).transpose(1, 0, 3, 2, 4).astype(jnp.float32)

    def step(state, qkv):
        qc, kc, vc = qkv
        inner = jnp.einsum('bhnm,bhmv->bhnv', jnp.einsum('bhnd,bhmd->bhnm', qc, kc) * d_in, vc)
        cross = jnp.einsum('bhnd,bhdv->bhnv', qc, state) * xi[None, :, :, None]
        state = state * chunk_decay[None, :, None, None] + jnp.einsum(
            'bhmd,bhmv->bhdv', kc * zeta[None, :, :, None], vc)
        return state, inner + cross

    state0 = jnp.zeros((B, H, dk, dv), jnp.float32)
    _, o = lax.scan(step, state0, (chunks(q), chunks(k), chunks(v)))
    o = o.transpose(1, 0, 3, 2, 4).reshape(B, S, H, dv)
    o = o * lax.rsqrt(jnp.mean(o * o, axis=-1, keepdims=True) + EPS)
    y = jax.nn.silu(gate.astype(jnp.float32)) * o.reshape(B, S, H * dv)
    return y.astype(xn.dtype) @ w_out

def t5_bucket(n):
    max_exact = NUM_BUCKETS // 2
    nf = jnp.maximum(n, max_exact).astype(jnp.float32)
    large = max_exact + (jnp.log(nf / max_exact) / math.log(MAX_DISTANCE / max_exact)
                         * (NUM_BUCKETS - max_exact)).astype(jnp.int32)
    large = jnp.minimum(large, NUM_BUCKETS - 1)
    return jnp.where(n < max_exact, n, large)

def dilated_group(q, k, v, bias_table, rate, n_steps):
    B, S, H, dh = q.shape
    Bk = SUB_BLOCK
    L = S // rate
    nb = -(-L // Bk)
    Lp = nb * Bk

    def to_blocks(t):
        t = t.reshape(B, L, rate, H, dh).transpose(0, 2, 1, 3, 4)
        t = jnp.pad(t, ((0, 0), (0, 0), (0, Lp - L), (0, 0), (0, 0)))
        return t.reshape(B, rate, nb, Bk, H, dh)

    def with_prev(t):
        prev = jnp.pad(t[:, :, :-1], ((0, 0), (0, 0), (1, 0), (0, 0), (0, 0), (0, 0)))
        return jnp.concatenate([prev, t], axis=3)

    qb = to_blocks(q)
    kk = with_prev(to_blocks(k))
    vv = with_prev(to_blocks(v))

    ql = jnp.arange(Bk, dtype=jnp.int32)[:, None]
    kl = jnp.arange(2 * Bk, dtype=jnp.int32)[None, :]
    steps = ql + Bk - kl
    bucket = t5_bucket(jnp.maximum(steps, 0) * rate)
    bias = bias_table[bucket].transpose(2, 0, 1).astype(jnp.float32)
    band = (steps >= 0) & (steps <= n_steps)
    first = (jnp.arange(nb) == 0)[:, None, None]
    valid = band[None] & ~(first & (kl < Bk)[None])

    s = jnp.einsum('brnqhd,brnkhd->brnhqk', qb, kk,
                   preferred_element_type=jnp.float32) * (dh ** -0.5) + bias[None, None, None]
    s = jnp.where(valid[None, None, :, None], s, NEG_INF)
    m = jnp.max(s, axis=-1)
    p = jnp.exp(s - m[..., None])
    l = jnp.sum(p, axis=-1)
    o = jnp.einsum('brnhqk,brnkhd->brnqhd', p, vv.astype(jnp.float32))

    def from_blocks(t):
        t = t.reshape((B, rate, Lp) + t.shape[4:])[:, :, :L]
        return jnp.moveaxis(t, 1, 2).reshape((B, S) + t.shape[3:])

    return (from_blocks(o), from_blocks(jnp.swapaxes(m, 3, 4)),
            from_blocks(jnp.swapaxes(l, 3, 4)))

def shared_kv(h, kv_norm, w_kv, k_norm):
    B, S, _ = h.shape
    kv = (rmsnorm(h, kv_norm) @ w_kv).reshape(B, S, 2, N_GROUPS, DIL_HEADS, DIL_HEAD_DIM)
    k = head_rmsnorm(kv[:, :, 0], k_norm[:, None, :])
    return k, kv[:, :, 1]

def dilated_attention(xn, k, v, w_q, q_norm, w_o, rel_bias):
    B, S, _ = xn.shape
    H, dh = DIL_HEADS, DIL_HEAD_DIM
    q = head_rmsnorm((xn @ w_q).reshape(B, S, N_GROUPS, H, dh), q_norm[:, None, :])
    outs, maxs, dens = [], [], []
    for g in range(N_GROUPS):
        o_g, m_g, l_g = dilated_group(q[:, :, g], k[:, :, g], v[:, :, g],
                                      rel_bias[:, g * H:(g + 1) * H],
                                      DIL_RATES[g], DIL_WINDOWS[g] // DIL_RATES[g])
        outs.append(o_g); maxs.append(m_g); dens.append(l_g)
    ms = jnp.stack(maxs)
    w = jnp.exp(ms - jnp.max(ms, axis=0, keepdims=True))
    num = jnp.sum(w[..., None] * jnp.stack(outs), axis=0)
    den = jnp.sum(w * jnp.stack(dens), axis=0)
    out = (num / den[..., None]).reshape(B, S, H * dh).astype(xn.dtype)
    return out @ w_o

def hier_moe(xt, w_grp, b_grp, w_exp, b_exp, w_gate, w_up, w_down):
    T, D = xt.shape
    grp_logits = (xt @ w_grp).astype(jnp.float32) + b_grp.astype(jnp.float32)
    grp = jnp.argmax(grp_logits, axis=-1)
    p_grp = jnp.take_along_axis(jax.nn.softmax(grp_logits, axis=-1), grp[:, None], axis=1)[:, 0]
    exp_logits = ((xt @ w_exp).astype(jnp.float32) + b_exp.astype(jnp.float32)).reshape(
        T, MOE_GROUPS, EXPERTS_PER_GROUP)
    in_grp = jnp.take_along_axis(exp_logits, grp[:, None, None], axis=1)[:, 0]
    top_v, top_i = lax.top_k(in_grp, TOP_K_INNER)
    gate = jax.nn.softmax(top_v, axis=-1) * p_grp[:, None]

    A = T * TOP_K_INNER
    eid = (grp[:, None] * EXPERTS_PER_GROUP + top_i).reshape(-1).astype(jnp.int32)
    tok = jnp.repeat(jnp.arange(T, dtype=jnp.int32), TOP_K_INNER)
    gw = gate.reshape(-1)
    order = jnp.argsort(eid)
    se = eid[order]
    counts = jnp.bincount(eid, length=N_EXPERTS).astype(jnp.int32)
    starts = jnp.cumsum(counts) - counts
    padded = (counts + MOE_BLOCK - 1) // MOE_BLOCK * MOE_BLOCK
    pends = jnp.cumsum(padded)
    pstarts = pends - padded
    dest = pstarts[se] + jnp.arange(A, dtype=jnp.int32) - starts[se]
    nblk = -(-A // MOE_BLOCK) + N_EXPERTS
    P = nblk * MOE_BLOCK
    rows_tok = jnp.full((P,), T, jnp.int32).at[dest].set(tok[order])
    rows_gate = jnp.zeros((P,), jnp.float32).at[dest].set(gw[order])
    blk_exp = jnp.minimum(jnp.searchsorted(pends, jnp.arange(nblk, dtype=jnp.int32) * MOE_BLOCK,
                                           side='right'), N_EXPERTS - 1)
    x_pad = jnp.concatenate([xt, jnp.zeros((1, D), xt.dtype)], axis=0)
    xb = x_pad[rows_tok].reshape(nblk, MOE_BLOCK, D)

    def expert_block(args):
        xk, e = args
        hid = jax.nn.silu(xk @ w_gate[e]) * (xk @ w_up[e])
        return hid @ w_down[e]

    yb = lax.map(expert_block, (xb, blk_exp)).reshape(P, D)
    y = jax.ops.segment_sum(yb * rows_gate[:, None].astype(yb.dtype), rows_tok,
                            num_segments=T + 1)
    return y[:T]

def setup_inputs(seed: int = 0) -> dict:
    key = jax.random.key(seed)
    ks = jax.random.split(key, 24)
    D = D_MODEL
    f32 = jnp.float32

    def w(k, shape, fan_in):
        return jax.random.normal(k, shape, f32) * (fan_in ** -0.5)

    def gain(k, shape):
        return 1.0 + 0.02 * jax.random.normal(k, shape, f32)

    ret_in_cols = 2 * RET_HEADS * RET_QK_DIM + 2 * RET_HEADS * RET_V_DIM
    q_cols = N_GROUPS * DIL_HEADS * DIL_HEAD_DIM
    return {
        "x": jax.random.normal(ks[0], (BATCH, SEQ, D), f32),
        "ret_w_in": w(ks[1], (N_A_LAYERS, D, ret_in_cols), D),
        "ret_w_out": w(ks[2], (N_A_LAYERS, RET_HEADS * RET_V_DIM, D), RET_HEADS * RET_V_DIM),
        "kv_norm": gain(ks[3], (D,)),
        "w_kv": w(ks[4], (D, 2 * q_cols), D),
        "k_norm": gain(ks[5], (N_GROUPS, DIL_HEAD_DIM)),
        "dil_wq": w(ks[6], (N_B_LAYERS, D, q_cols), D),
        "q_norm": gain(ks[7], (N_B_LAYERS, N_GROUPS, DIL_HEAD_DIM)),
        "dil_wo": w(ks[8], (N_B_LAYERS, DIL_HEADS * DIL_HEAD_DIM, D), DIL_HEADS * DIL_HEAD_DIM),
        "rel_bias": 0.2 * jax.random.normal(ks[9], (NUM_BUCKETS, N_GROUPS * DIL_HEADS), f32),
        "mixer_norm": gain(ks[10], (DEPTH, D)),
        "ffn_norm": gain(ks[11], (DEPTH, D)),
        "router_grp": w(ks[12], (DEPTH, D, MOE_GROUPS), D),
        "router_grp_b": 0.01 * jax.random.normal(ks[13], (DEPTH, MOE_GROUPS), f32),
        "router_exp": w(ks[14], (DEPTH, D, N_EXPERTS), D),
        "router_exp_b": 0.01 * jax.random.normal(ks[15], (DEPTH, N_EXPERTS), f32),
        "exp_gate": w(ks[16], (DEPTH, N_EXPERTS, D, EXPERT_FF), D),
        "exp_up": w(ks[17], (DEPTH, N_EXPERTS, D, EXPERT_FF), D),
        "exp_down": w(ks[18], (DEPTH, N_EXPERTS, EXPERT_FF, D), EXPERT_FF),
    }

def reference(x, ret_w_in, ret_w_out, kv_norm, w_kv, k_norm, dil_wq, q_norm, dil_wo, rel_bias,
              mixer_norm, ffn_norm, router_grp, router_grp_b, router_exp, router_exp_b,
              exp_gate, exp_up, exp_down):
    B, S, D = x.shape
    h = x
    k_sh, v_sh = None, None
    for layer in range(DEPTH):
        xn = rmsnorm(h, mixer_norm[layer])
        if layer < N_A_LAYERS:
            mix = retention(xn, ret_w_in[layer], ret_w_out[layer])
        else:
            j = layer - N_A_LAYERS
            if j == 0:
                k_sh, v_sh = shared_kv(h, kv_norm, w_kv, k_norm)
            mix = dilated_attention(xn, k_sh, v_sh, dil_wq[j], q_norm[j], dil_wo[j], rel_bias)
        h = h + mix
        hn = rmsnorm(h, ffn_norm[layer]).reshape(B * S, D)
        h = h + hier_moe(hn, router_grp[layer], router_grp_b[layer], router_exp[layer],
                         router_exp_b[layer], exp_gate[layer], exp_up[layer],
                         exp_down[layer]).reshape(B, S, D)
    return h


_drawn_inputs = setup_inputs


def setup_inputs(seed=0):
    import zlib

    import numpy as np

    out = dict(_drawn_inputs(seed))
    spreads = {}
    factors = {'kv_norm': 6.768,
     'k_norm': 5.581,
     'q_norm': 8.0,
     'router_grp_b': 4.028,
     'router_exp_b': 3.934}
    for name, (base, spread) in spreads.items():
        noise = np.random.default_rng([zlib.crc32(name.encode()), seed]).standard_normal(out[name].shape)
        drawn = base * np.exp(spread * noise) if base else spread * noise
        out[name] = __import__('jax').numpy.asarray(drawn.astype(out[name].dtype))
    for name, factor in factors.items():
        out[name] = (out[name] * factor).astype(out[name].dtype)
    return out
```

```python
from contextlib import ExitStack

import numpy as np

import concourse.bass as bass
from concourse import mybir

F32 = mybir.dt.float32
F32R = mybir.dt.float32r
I32 = mybir.dt.int32
ALU = mybir.AluOpType
ACT = mybir.ActivationFunctionType
AX = mybir.AxisListType.X

P = 128
D = 1024
S = 256
TT = S // P
KD = D // P
RET_H = 4
RET_DK = D // RET_H
RET_DV = 2 * RET_DK
RET_KO = RET_H * RET_DV // P
GROUPS = 3
RATES = (1, 4, 16)
WINDOWS = (128, 512, 2048)
DIL_H = 16
DIL_DH = D // DIL_H
QCOLS = GROUPS * DIL_H * DIL_DH
BUCKETS = 32
MAX_DISTANCE = 2048
MG = 4
EPG = 8
NE = MG * EPG
FF = D // 2
EPS = 1e-6
FAR = 1e30

RING = 9
FULL_RING = 6
DENSE_RING = 4
WORK = 18432
TILE = 4096
COLS = TILE // KD
SLOTS = 32
PER_GROUP = P // SLOTS
EXPERT_GROUPS = NE // PER_GROUP
MOE_TILES = 3 * 4
MAX_OVERFLOW = 16

MOE_SLOT = (6, 7, 0, 1, 2, 3, 4, 5, 8, 6, 7, 8)

N_WIN, N_WOUT, N_KV, N_WO = 12, 4, 6, 2
FIRST_WIN = 0
FIRST_WOUT = FIRST_WIN + N_WIN
FIRST_MOE = [FIRST_WOUT + N_WOUT]
FIRST_QKV = FIRST_MOE[0] + MOE_TILES * EXPERT_GROUPS
FIRST_WO = FIRST_QKV + 3 * N_KV
FIRST_MOE.append(FIRST_WO + N_WO)

DENSE_A = N_WIN + N_WOUT
DENSE_B = 3 * N_KV + N_WO

C_IDENT = 0
C_TRI = C_IDENT + P
C_ONES = C_TRI + P
C_IOTA = C_ONES + P
C_KEPT = C_IOTA + P
C_COS = C_KEPT
C_SIN = C_COS + S
C_DECAY = C_SIN + S
DECAY_W = S + P
C_BUCKET = C_DECAY + RET_H * DECAY_W
BW = 384
C_MASK = C_BUCKET + BW
C_ALL = C_MASK + BW


def shape_constants():
    c = np.zeros((P, C_ALL), np.float32)
    p = np.arange(P)
    c[:, C_IDENT:C_IDENT + P] = np.eye(P)
    c[:, C_TRI:C_TRI + P] = p[:, None] < p[None, :]
    c[:, C_ONES:C_ONES + P] = 1.0
    c[:, C_IOTA:C_IOTA + P] = p[None, :]
    half = RET_DK // 2
    inv = (1.0 / (np.float32(10000.0) ** np.linspace(0.0, 1.0, half, dtype=np.float32))).astype(np.float32)
    ang = (np.arange(S, dtype=np.float32)[None, :] * inv[:, None]).astype(np.float32)
    c[:, C_COS:C_COS + S] = np.cos(ang)
    c[:, C_SIN:C_SIN + S] = np.sin(ang)
    for h in range(RET_H):
        log_g = np.log(1.0 - 2.0 ** (-5.0 - h))
        diff = np.arange(S)[None, :] - p[:, None]
        dec = np.where(diff >= 0, np.exp(log_g * np.maximum(diff, 0)), 0.0) * RET_DK ** -0.5
        at = C_DECAY + h * DECAY_W
        c[:, at:at + S] = dec
        c[:, at + S:at + DECAY_W] = dec[:, :P]
    dist = S - 1 - np.arange(BW)
    exact = BUCKETS // 2
    n = np.maximum(dist, 0)
    nf = np.maximum(n, exact).astype(np.float32)
    large = exact + (np.log(nf / exact) / np.float32(np.log(MAX_DISTANCE / exact))
                     * (BUCKETS - exact)).astype(np.int32)
    bucket = np.where(n < exact, n, np.minimum(large, BUCKETS - 1))
    c[:BUCKETS, C_BUCKET:C_BUCKET + BW] = np.arange(BUCKETS)[:, None] == bucket[None, :]
    for g, (rate, window) in enumerate(zip(RATES, WINDOWS)):
        seen = (dist >= 0) & (dist % rate == 0) & (dist <= window)
        c[g * DIL_H:(g + 1) * DIL_H, C_MASK:C_MASK + BW] = np.where(seen, 0.0, -FAR)[None, :]
    return c


class Chain:

    def __init__(self, engine, sem, base=0):
        self.engine, self.sem, self.base, self.n = engine, sem, base, 0

    def __call__(self, instruction):
        instruction.then_inc(self.sem, 1)
        self.n += 1
        self.engine.wait_ge(self.sem, self.base + self.n)


DVE_PER_GROUP = 3


def build(nc, x, ret_w_in, ret_w_out, kv_norm, w_kv, k_norm, dil_wq, q_norm, dil_wo, rel_bias,
          mixer_norm, ffn_norm, router_grp, router_grp_b, router_exp, router_exp_b,
          exp_gate, exp_up, exp_down, constants, out):
    bias_rows = nc.dram_tensor("bias_rows", (GROUPS * DIL_H, BW), F32, kind="Internal").ap()
    ctx = ExitStack()
    with ctx:
        def sb(name, shape, dt=F32):
            return ctx.enter_context(nc.sbuf_tensor(name, shape, dt))

        def sem(name):
            return ctx.enter_context(nc.semaphore(name))

        arena_at = (nc.sbuf_base + 31) // 32 * 32
        sb("arena", [P, FULL_RING * TILE + 4 * TT * D + WORK])
        HN_AT = FULL_RING * TILE
        XT_AT = HN_AT + TT * D
        XT2_AT = XT_AT + KD * S
        H_AT = XT2_AT + KD * S
        WORK_AT = H_AT + TT * D

        def place(name, word, shape, dt=F32):
            return nc.alloc_sbuf_tensor_at(name, shape, dt, offset=arena_at + 4 * word)

        ring = place("ring", 0, [P, FULL_RING, TILE])
        ring_more = place("ring_more", WORK_AT + TILE, [P, RING - FULL_RING, TILE])
        ring_lo = place("ring_lo", 0, [P, DENSE_RING, TILE], F32R)
        ring_hi = place("ring_hi", DENSE_RING * TILE, [P, 2, TILE], F32R)
        h = place("h", H_AT, [P, TT, D])
        hn = place("hn", HN_AT, [P, TT, D])
        xT = place("xT", XT_AT, [P, KD, S])
        work = place("work", WORK_AT, [P, WORK])
        x_hi = place("x_hi", XT_AT, [P, KD, S], F32R)
        x_lo = place("x_lo", XT2_AT, [P, KD, S], F32R)
        xq_hi = place("xq_hi", WORK_AT + 12288, [P, KD, S], F32R)
        xq_lo = place("xq_lo", WORK_AT + 12288 + KD * S, [P, KD, S], F32R)
        yT_hi = place("yT_hi", WORK_AT + 12288, [P, RET_KO, S], F32R)
        yT_lo = place("yT_lo", WORK_AT, [P, RET_KO, S], F32R)
        aT_hi = place("aT_hi", WORK_AT, [P, KD, S], F32R)
        aT_lo = place("aT_lo", WORK_AT + KD * S, [P, KD, S], F32R)
        xT2 = place("xT2", XT2_AT, [P, KD, S])
        kept = sb("kept", [P, C_KEPT])
        gains = sb("gains", [P, 5, KD])
        qk_gain = sb("qk_gain", [P, 2, GROUPS])
        w_route = sb("w_route", [P, KD, MG + NE])
        b_route = sb("b_route", [P, MG + NE])
        stat = sb("stat", [P, 3, 2 * RET_H])
        root_of_no_use = sb("root_of_no_use", [P, 4])
        rt = sb("rt", [P, 512])
        slot_of = sb("slot_of", [P, 2, TT])
        gate_of = sb("gate_of", [P, 2, TT])
        blocks = sb("blocks", [P, MAX_OVERFLOW + 1], I32)
        bank = [ctx.enter_context(nc.psum_tensor(f"bank{i}", [P, 512], F32))[:, :] for i in range(2)]
        pair = ctx.enter_context(nc.psum_tensor("pair", [P, 1024], F32))
        bank += [pair[:, 0:512], pair[:, 512:1024]]
        bank += [ctx.enter_context(nc.psum_tensor(f"bank{i}", [P, 512], F32))[:, :] for i in range(4, 8)]

        ident = kept[:, C_IDENT:C_IDENT + P]
        tri = kept[:, C_TRI:C_TRI + P]
        ones = kept[:, C_ONES:C_ONES + P]
        iota = kept[:, C_IOTA:C_IOTA + P]

        def area(at, *shape):
            size = int(np.prod(shape))
            v = work[:, at:at + size]
            if len(shape) == 2:
                return v.rearrange("p (a b) -> p a b", b=shape[1])
            if len(shape) == 3:
                return v.rearrange("p (a b c) -> p a b c", b=shape[1], c=shape[2])
            return v

        def dense_slot(n):
            return (n - (0 if n < FIRST_MOE[0] else FIRST_QKV)) % DENSE_RING

        def moe_slot(j):
            at = MOE_SLOT[j]
            return ring[:, at, :] if at < FULL_RING else ring_more[:, at - FULL_RING, :]

        def loads_before(layer, at):
            dense = (DENSE_A, DENSE_A + DENSE_B)[layer] // DENSE_RING if at < DENSE_RING else 0
            return dense + layer * MOE_SLOT.count(at) * EXPERT_GROUPS

        s_small = sem("small_loaded")
        s_x = sem("x_loaded")
        s_ring = [sem(f"ring_loaded{i}") for i in range(RING)]
        s_used = sem("ring_tiles_used")
        s_sq = sem("squares_summed")
        s_var = sem("variance_ready")
        s_std = sem("std_ready")
        s_hn = sem("hn_ready")
        s_tp = sem("transposed")
        s_xT = sem("xT_ready")
        s_dv = sem("dve_step")
        s_h = sem("h_updated")
        s_out = sem("out_stored")

        s_hi = sem("weight_halves_hi")
        s_lo = sem("weight_halves_lo")

        def load_tile(sp, n, src, parts):
            i = n if n < FIRST_MOE[0] else n - FIRST_QKV
            if i >= DENSE_RING:
                sp.wait_ge(s_used, n - DENSE_RING + 1)
            elif n >= FIRST_QKV:
                sp.wait_ge(s_used, FIRST_QKV - MOE_TILES + MOE_SLOT.index(i) + 1)
            at = dense_slot(n)
            sp.dma_start(ring[:, at, :].rearrange("p (a b) -> p a b", a=parts), src).then_inc(s_ring[at], 16)

        def dense_index(n):
            return n if n < FIRST_MOE[0] else n - FIRST_QKV + DENSE_A

        def split_act(act, n):
            d = dense_index(n)
            loads = dense_index(n) // DENSE_RING + 1
            if n >= FIRST_QKV:
                loads += MOE_SLOT.count(dense_slot(n)) * EXPERT_GROUPS
            act.wait_ge(s_ring[dense_slot(n)], 16 * loads)
            if n in (FIRST_QKV, FIRST_QKV + 1):
                act.wait_ge(s_used, FIRST_QKV)
            elif d >= 2:
                act.wait_ge(s_used, n - 1)
            for half in range(2):
                cols = slice(half * TILE // 2, (half + 1) * TILE // 2)
                nc.scalar.copy(ring_hi[:, d % 2, cols], ring[:, dense_slot(n), cols]).then_inc(s_hi, 1)

        def split_dve(dve, n):
            d = dense_index(n)
            for half in range(2):
                cols = slice(half * TILE // 2, (half + 1) * TILE // 2)
                dve.wait_ge(s_hi, 2 * d + half + 1)
                nc.vector.tensor_tensor(ring_lo[:, dense_slot(n), cols], ring[:, dense_slot(n), cols],
                                        ring_hi[:, d % 2, cols].bitcast(F32), ALU.subtract).then_inc(s_lo, 1)

        def split_next(split, engine, n, last):
            if n + 2 <= last:
                split(engine, n + 2)

        def halves(n, k):
            d = dense_index(n)
            return (ring_hi[:, d % 2, :].rearrange("p (k c) -> p k c", k=k),
                    ring_lo[:, dense_slot(n), :].rearrange("p (k c) -> p k c", k=k))

        def half_ready(pe, n, half):
            pe.wait_ge(s_lo, 2 * dense_index(n) + half + 1)

        def three_passes(out, left, right, first, last):
            nc.tensor.matmul(out, left[0], right[0], start=first, stop=False)
            nc.tensor.matmul(out, left[0], right[1], start=False, stop=False)
            return nc.tensor.matmul(out, left[1], right[0], start=False, stop=last)

        win = ret_w_in[0].rearrange("(p k) n -> p k n", k=KD)
        wout = ret_w_out[0].rearrange("(p k) n -> p k n", k=RET_KO)
        wkv = w_kv.rearrange("(p k) n -> p k n", k=KD)
        wq = dil_wq[0].rearrange("(p k) n -> p k n", k=KD)
        wo = dil_wo[0].rearrange("(p k) n -> p k n", k=KD)

        NORMS = {"mix0": 0, "ffn0": 1, "mix1": 2, "ffn1": 3}
        HS = {"mix0": 0, "ffn0": 4, "mix1": 0, "ffn1": 4}

        def norm_act(act, i):
            if i == 0:
                act.wait_ge(s_x, 16)
            elif i == 2:
                act.wait_ge(s_h, H_DONE[i])
                act.wait_ge(m[0]["over"]["h_added"], 4 * overflow_blocks(act, 0) + 1)
            else:
                act.wait_ge(s_h, H_DONE[i] - 2)
            for t in range(TT if i == 2 else 1):
                nc.scalar.activation(hn[:, t, :], h[:, t, :], ACT.Square,
                                     accum_out=stat[:, 0, t:t + 1]).then_inc(s_sq, 1)
            if i != 2:
                nc.scalar.activation(root_of_no_use[0:1, i:i + 1], h[0:1, 0, 0:1], ACT.Sqrt, scale=0.0)
            act.wait_ge(s_var, i + 1)
            nc.scalar.activation(stat[:, 2, 0:TT], stat[:, 1, 0:TT], ACT.Sqrt).then_inc(s_std, 1)

        def norm_dve(dve, chain, i):
            if i == 0:
                dve.wait_ge(s_x, 16)
            elif i != 2:
                dve.wait_ge(s_h, H_DONE[i])
            if i != 2:
                nc.vector.tensor_tensor_reduce(out=hn[:, 1, :], in0=h[:, 1, :], in1=h[:, 1, :], scale=1.0,
                                               scalar=0.0, op0=ALU.mult, op1=ALU.add,
                                               accum_out=stat[:, 0, 1:2]).then_inc(s_sq, 1)
            dve.wait_ge(s_sq, TT * (i + 1))
            nc.vector.tensor_scalar(stat[:, 1, 0:TT], stat[:, 0, 0:TT], 1.0 / D, EPS,
                                    ALU.mult, ALU.add).then_inc(s_var, 1)
            dve.wait_ge(s_std, i + 1)
            chain(nc.vector.reciprocal(stat[:, 1, 0:TT], stat[:, 2, 0:TT]))
            for t in range(TT):
                nc.vector.tensor_scalar(hn[:, t, :], h[:, t, :], stat[:, 1, t:t + 1], None,
                                        ALU.mult).then_inc(s_hn, 1)

        SPLIT_NORMS = (0, 2)
        tp_bank = (bank[0], bank[1], bank[6], bank[7])
        s_xT_act = sem("xT_batches_by_act")
        s_xT_dve = sem("xT_batches_by_dve")

        def batches_done(i, b, by_act):
            before = sum(4 if j in SPLIT_NORMS else 2 for j in range(i))
            return before + (b + 1 if i in SPLIT_NORMS else b // 2 + 1)

        def transpose_pe(pe, i):
            pe.wait_ge(s_hn, TT * (i + 1))
            for b in range(KD // 2):
                for kk in range(2):
                    for t in range(TT):
                        k = 2 * b + kk
                        col = (kk * TT + t) * P
                        last = nc.tensor.transpose(tp_bank[b][:, col:col + P], hn[:, t, k::KD], ident)
                last.then_inc(s_tp, 1)

        def transpose_act(act, i, outs):
            for b in range(4) if i in SPLIT_NORMS else (0, 2):
                act.wait_ge(s_tp, 4 * i + b + 1)
                for kk in range(2):
                    k = 2 * b + kk
                    for o, g in outs:
                        o = o[0] if i in SPLIT_NORMS else o
                        last = nc.scalar.mul(o[:, k, :], tp_bank[b][:, kk * S:(kk + 1) * S],
                                             gains[:, g, k:k + 1])
                last.then_inc(s_xT_act, 1)

        def transpose_dve(dve, i, outs):
            for b in range(4) if i in SPLIT_NORMS else (1, 3):
                dve.wait_ge(s_tp, 4 * i + b + 1)
                if i in SPLIT_NORMS:
                    dve.wait_ge(s_xT_act, batches_done(i, b, True))
                for kk in range(2):
                    k = 2 * b + kk
                    src = tp_bank[b][:, kk * S:(kk + 1) * S]
                    for o, g in outs:
                        if i in SPLIT_NORMS:
                            last = nc.vector.scalar_tensor_tensor(
                                out=o[1][:, k, :], in0=src, scalar=gains[:, g, k:k + 1],
                                in1=o[0][:, k, :].bitcast(F32), op0=ALU.mult, op1=ALU.subtract)
                        else:
                            last = nc.vector.tensor_scalar(o[:, k, :], src, gains[:, g, k:k + 1], None, ALU.mult)
                last.then_inc(s_xT_dve, 1)

        def xT_ready(engine, i):
            if i not in SPLIT_NORMS:
                engine.wait_ge(s_xT_act, batches_done(i, 2, True))
            engine.wait_ge(s_xT_dve, batches_done(i, 3, False))

        H_DONE = {1: 4, 2: 4 + 4 * EXPERT_GROUPS, 3: 8 + 4 * EXPERT_GROUPS, 4: 8 + 8 * EXPERT_GROUPS}
        ATTN_H0 = H_DONE[2]
        MOE_H0 = [H_DONE[1], H_DONE[3]]

        r_q = area(0, RET_H, 2, S)
        r_k = area(2048, RET_H, 2, S)
        r_v = area(4096, TT, RET_H * RET_DV)
        r_y = area(8192, TT, RET_H * RET_DV)
        r_cos = work[:, 16384:16384 + S]
        r_sin = work[:, 16640:16640 + S]
        r_dec = area(16896, RET_H, DECAY_W)
        r_a = hn[:, 0, 0:2 * DECAY_W].rearrange("p (b n) -> p b n", b=2)
        r_sg = hn[:, 1, :].rearrange("p (b n) -> p b n", b=2)
        r_ta = hn[:, 0, 0:2 * S].rearrange("p (a s) -> p a s", a=2)
        r_tb = hn[:, 0, 2 * S:4 * S].rearrange("p (a s) -> p a s", a=2)
        r_sq = rt[:, 0:RET_DV]
        r_tab = sem("retention_tables_loaded")
        r_qk_done = sem("ret_qk_projected")
        r_rope = sem("ret_qk_rotated")
        r_vg_done = sem("ret_vg_projected")
        r_v_act = sem("ret_v_kept_by_act")
        r_v_dve = sem("ret_v_kept_by_dve")
        r_s_done = sem("ret_scores")
        r_a_ready = sem("ret_scores_decayed")
        r_o_done = sem("ret_heads_out")
        r_o_kept = sem("ret_heads_out_kept")
        r_sumsq = sem("ret_head_squares")
        r_var = sem("ret_head_variance")
        r_std = sem("ret_head_std")
        r_sg_ready = sem("ret_silu_ready")
        r_y_ready = sem("ret_y_ready")
        r_yt_done = sem("ret_y_transposed")
        r_yt_act = sem("ret_yT_by_act")
        r_yt_dve = sem("ret_yT_by_dve")
        r_out_done = sem("ret_out_projected")

        def backwards(view):
            size = view.shape[2]
            return bass.AP(view.tensor, view.offset + size - 1, [view.ap[0], view.ap[1], [-1, size]])

        def retention_pe(pe):
            xT_ready(pe, 0)
            for n in range(4):
                w = halves(n, KD)
                for hh in range(2):
                    i = 2 * n + hh
                    if i >= 4:
                        pe.wait_ge(r_rope, i - 3)
                    for half in range(2):
                        for k in range(KD):
                            c = (2 * hh + half) * P
                            if hh == 0 and half == 0 and k % 4 == 0:
                                half_ready(pe, n, k // 4)
                            last = three_passes(bank[2 + i % 4][:, half * S:(half + 1) * S],
                                                [v[:, k, c:c + P] for v in w],
                                                (x_hi[:, k, :], x_lo[:, k, :]), k == 0, k == KD - 1)
                    if hh == 0:
                        last.then_inc(r_qk_done, 1)
                last.then_inc(s_used, 1)
            bias_pe(pe)
            project_natural(pe, range(4, 8), r_vg_done, r_v_act, r_v_dve)
            for hd in range(RET_H):
                if hd == 0:
                    pe.wait_ge(r_rope, 8)
                if hd >= 2:
                    pe.wait_ge(r_a_ready, hd - 1)
                sc = bank[hd % 2]
                for half in range(2):
                    nc.tensor.matmul(sc[:, 0:S], r_k[:, hd, half, 0:P], r_q[:, hd, half, :],
                                     start=(half == 0), stop=(half == 1))
                for half in range(2):
                    last = nc.tensor.matmul(sc[:, S:S + P], r_k[:, hd, half, P:S], r_q[:, hd, half, P:S],
                                            start=(half == 0), stop=(half == 1))
                last.then_inc(r_s_done, 1)
                if hd >= 1:
                    retention_pv(pe, hd - 1)
            retention_pv(pe, RET_H - 1)
            pe.wait_ge(r_o_kept, 2 * RET_H)
            for n in range(8, 12):
                for t in range(TT):
                    i = 2 * (n - 8) + t
                    if i >= 4:
                        pe.wait_ge(r_sg_ready, i - 3)
                    last = project(pe, bank[2 + i % 4], (x_hi, x_lo), n, t)
                    if t == 0:
                        last.then_inc(r_vg_done, 1)
                last.then_inc(s_used, 1)
            for b in range(RET_KO // 2):
                if b == 0:
                    pe.wait_ge(r_y_ready, 2 * RET_H)
                if b >= 2:
                    pe.wait_ge(r_yt_dve, b - 1)
                for kk in range(2):
                    for t in range(TT):
                        col = (kk * TT + t) * P
                        last = nc.tensor.transpose(bank[b % 2][:, col:col + P], r_y[:, t, 2 * b + kk::RET_KO],
                                                   ident)
                last.then_inc(r_yt_done, 1)
            pe.wait_ge(r_yt_dve, RET_KO // 2)
            project_out(pe, FIRST_WOUT, N_WOUT, 4, (yT_hi, yT_lo), r_out_done)

        def project(pe, out, x, n, t):
            w = halves(n, KD)
            rows = slice(t * P, (t + 1) * P)
            for k in range(KD):
                if t == 0 and k % 4 == 0:
                    half_ready(pe, n, k // 4)
                last = three_passes(out, [v[:, k, rows] for v in x], [v[:, k, :] for v in w],
                                    k == 0, k == KD - 1)
            return last

        def project_natural(pe, tiles, done, by_act, by_dve):
            for i, n in enumerate(tiles):
                for t in range(TT):
                    if i >= 2:
                        pe.wait_ge((by_act, by_dve)[t], i - 1)
                    elif i == 0 and t == 0:
                        pe.wait_ge(r_rope, 8)
                    last = project(pe, bank[2 + 2 * (i % 2) + t], (x_hi, x_lo), n, t)
                    if t == 0:
                        last.then_inc(done, 1)
                last.then_inc(s_used, 1)

        def retention_pv(pe, hd):
            pe.wait_ge(r_a_ready, hd + 1)
            if hd == 0:
                pe.wait_ge(r_v_act, 4)
                pe.wait_ge(r_v_dve, 4)
            if hd >= 2:
                pe.wait_ge(r_o_kept, 2 * (hd - 1))
            a = r_a[:, hd % 2, :]
            cols = slice(hd * RET_DV, (hd + 1) * RET_DV)
            o = [bank[2 + 2 * (hd % 2) + t] for t in range(TT)]
            nc.tensor.matmul(o[0], a[:, 0:P], r_v[:, 0, cols], start=True, stop=True).then_inc(r_o_done, 1)
            nc.tensor.matmul(o[1], a[:, P:S], r_v[:, 0, cols], start=True, stop=False)
            nc.tensor.matmul(o[1], a[:, S:S + P], r_v[:, 1, cols], start=False, stop=True).then_inc(r_o_done, 1)

        def project_out(pe, first, tiles, rows, lhs, done):
            kt = tiles * rows
            for j in range(tiles):
                w = halves(first + j, rows)
                for r in range(rows):
                    k = j * rows + r
                    if r % (rows // 2) == 0:
                        half_ready(pe, first + j, r // (rows // 2))
                    for t in range(TT):
                        for nh in range(2):
                            last = three_passes(bank[2 + 2 * t + nh],
                                                [v[:, k, t * P:(t + 1) * P] for v in lhs],
                                                [v[:, r, nh * 512:(nh + 1) * 512] for v in w],
                                                k == 0, k == kt - 1)
                            if k == kt - 1 and (t, nh) != (1, 1):
                                last.then_inc(done, 1)
                last.then_inc(s_used, 1)

        def add_out_dve(dve, first, tiles, done):
            for t in range(TT):
                for nh in range(2):
                    i = 2 * t + nh
                    if i < 3:
                        dve.wait_ge(done, i + 1)
                    else:
                        dve.wait_ge(s_used, first + tiles)
                    hs = h[:, t, nh * 512:(nh + 1) * 512]
                    nc.vector.tensor_tensor(hs, hs, bank[2 + i], ALU.add).then_inc(s_h, 1)

        def retention_act(act):
            for n in range(-2, 4):
                split_next(split_act, act, n, DENSE_A - 1)
            for i in range(4):
                act.wait_ge(r_vg_done, i + 1)
                nc.scalar.copy(r_v[:, 0, i * 512:(i + 1) * 512], bank[2 + 2 * (i % 2)]).then_inc(r_v_act, 1)
                split_next(split_act, act, 4 + i, DENSE_A - 1)
            for i in range(2 * RET_H):
                act.wait_ge(r_o_kept, i + 1)
                if i >= 1:
                    act.wait_ge(r_sumsq, i)
                hd, t = i // 2, i % 2
                nc.scalar.activation(r_sq, r_y[:, t, hd * RET_DV:(hd + 1) * RET_DV], ACT.Square,
                                     accum_out=stat[:, 0, i:i + 1]).then_inc(r_sumsq, 1)
            act.wait_ge(r_var, 1)
            nc.scalar.activation(stat[:, 2, :], stat[:, 1, :], ACT.Sqrt).then_inc(r_std, 1)
            for i in range(2 * RET_H):
                hd, t = i // 2, i % 2
                if t == 0:
                    act.wait_ge(r_vg_done, 4 + hd + 1)
                else:
                    act.wait_ge(s_used, 8 + hd + 1)
                if i >= 2:
                    act.wait_ge(r_y_ready, i - 1)
                nc.scalar.activation(r_sg[:, i % 2, :], bank[2 + i % 4], ACT.Silu).then_inc(r_sg_ready, 1)
                if t == 1:
                    split_next(split_act, act, 8 + hd, DENSE_A - 1)
            act.wait_ge(b_stored, 16)
            for b in range(RET_KO // 2):
                act.wait_ge(r_yt_done, b + 1)
                nc.scalar.copy(yT_hi[:, 2 * b:2 * b + 2, :],
                               bank[b % 2].rearrange("p (k s) -> p k s", k=2)).then_inc(r_yt_act, 1)
            for n in range(FIRST_WOUT, FIRST_WOUT + N_WOUT):
                split_next(split_act, act, n, DENSE_A - 1)

        def retention_dve(dve, chain):
            for n in range(-2, 0):
                split_next(split_dve, dve, n, DENSE_A - 1)
            dve.wait_ge(r_tab, 16 * 3)
            for i in range(8):
                if i % 2 == 0:
                    dve.wait_ge(r_qk_done, i // 2 + 1)
                else:
                    dve.wait_ge(s_used, i // 2 + 1)
                src = bank[2 + i % 4].rearrange("p (a s) -> p a s", a=2)
                dst = (r_q if i < 4 else r_k)[:, i % 4, :, :]
                cos = r_cos.unsqueeze(1).to_broadcast([P, 2, S])
                sin = r_sin.unsqueeze(1).to_broadcast([P, 2, S])
                nc.vector.tensor_tensor(r_ta, src, cos, ALU.mult)
                chain(nc.vector.tensor_tensor(r_tb, src, sin, ALU.mult))
                nc.vector.tensor_tensor(dst[:, 0, :], r_ta[:, 0, :], r_tb[:, 1, :], ALU.subtract)
                nc.vector.tensor_tensor(dst[:, 1, :], r_tb[:, 0, :], r_ta[:, 1, :], ALU.add).then_inc(r_rope, 1)
                dve.wait_ge(r_rope, i + 1)
                if i % 2 == 1:
                    split_next(split_dve, dve, i // 2, DENSE_A - 1)
            bias_dve(dve)
            for i in range(4):
                dve.wait_ge(s_used, 4 + i + 1)
                nc.vector.tensor_copy(r_v[:, 1, i * 512:(i + 1) * 512],
                                      bank[3 + 2 * (i % 2)]).then_inc(r_v_dve, 1)
                split_next(split_dve, dve, 4 + i, DENSE_A - 1)
            for hd in range(RET_H):
                dve.wait_ge(r_s_done, hd + 1)
                if hd >= 2:
                    dve.wait_ge(r_o_done, 2 * (hd - 1))
                nc.vector.tensor_tensor(r_a[:, hd % 2, :], bank[hd % 2][:, 0:DECAY_W], r_dec[:, hd, :],
                                        ALU.mult).then_inc(r_a_ready, 1)
                if hd >= 1:
                    keep_heads(dve, hd - 1)
            keep_heads(dve, RET_H - 1)
            dve.wait_ge(r_sumsq, 2 * RET_H)
            nc.vector.tensor_scalar(stat[:, 1, :], stat[:, 0, :], 1.0 / RET_DV, EPS,
                                    ALU.mult, ALU.add).then_inc(r_var, 1)
            dve.wait_ge(r_std, 1)
            chain(nc.vector.reciprocal(stat[:, 1, :], stat[:, 2, :]))
            for i in range(2 * RET_H):
                hd, t = i // 2, i % 2
                dve.wait_ge(r_sg_ready, i + 1)
                y = r_y[:, t, hd * RET_DV:(hd + 1) * RET_DV]
                nc.vector.scalar_tensor_tensor(out=y, in0=y, scalar=stat[:, 1, i:i + 1], in1=r_sg[:, i % 2, :],
                                               op0=ALU.mult, op1=ALU.mult).then_inc(r_y_ready, 1)
                if t == 1:
                    split_next(split_dve, dve, 8 + hd, DENSE_A - 1)
            for b in range(RET_KO // 2):
                dve.wait_ge(r_yt_act, b + 1)
                nc.vector.tensor_tensor(yT_lo[:, 2 * b:2 * b + 2, :],
                                        bank[b % 2].rearrange("p (k s) -> p k s", k=2),
                                        yT_hi[:, 2 * b:2 * b + 2, :].bitcast(F32),
                                        ALU.subtract).then_inc(r_yt_dve, 1)
            for n in range(FIRST_WOUT, FIRST_WOUT + N_WOUT):
                split_next(split_dve, dve, n, DENSE_A - 1)
            add_out_dve(dve, FIRST_WOUT, N_WOUT, r_out_done)

        def keep_heads(dve, hd):
            for t in range(TT):
                dve.wait_ge(r_o_done, 2 * hd + t + 1)
                nc.vector.tensor_copy(r_y[:, t, hd * RET_DV:(hd + 1) * RET_DV],
                                      bank[2 + 2 * (hd % 2) + t]).then_inc(r_o_kept, 1)

        m_sel = area(0, TT, P)
        m_gsel = area(256, TT, P)
        m_gselT = work[:, 512:768]
        m_x = area(1024, KD, P)
        m_sg = work[:, 2048:2560]
        m_hid = work[:, 2560:3072]
        m_hidT = work[:, 3072:3584]
        m_y = work[:, 16384:17408]
        m_t = area(17408, 2, P)
        m = []
        for layer in range(2):
            names = ("logits", "exp_in", "exp_out", "top_in", "top_out", "chosen", "ranked", "slots_ready",
                     "route_w", "step")
            main = ("sel_ready", "gathered", "x_ready", "gselT_done", "gselT_ready", "silu_ready", "hid_ready",
                    "hidT_done", "hidT_ready", "y_done", "y_ready", "combined", "dve")
            over = main + ("used", "h_added", "loaded0", "loaded1", "loaded2")
            m.append({
                **{n: sem(f"moe{layer}_{n}") for n in names},
                "main": {n: sem(f"moe{layer}_group_{n}") for n in main},
                "over": {n: sem(f"moe{layer}_overflow_{n}") for n in over},
            })

        def last_user(j):
            earlier = [i for i in range(-MOE_TILES, j) if MOE_SLOT[i % MOE_TILES] == MOE_SLOT[j]]
            return earlier[-1]

        def free_work_slots(sp, layer, at):
            if layer == 0:
                sp.wait_ge(s_used, FIRST_WOUT + 1)
            else:
                sp.wait_ge(a_sc, 2 * DIL_H)

        def moe_sp(sp, layer):
            first = FIRST_MOE[layer]
            rows = {"gate": exp_gate[layer].rearrange("e (p k) f -> p e (k f)", k=KD),
                    "up": exp_up[layer].rearrange("e (p k) f -> p e (k f)", k=KD),
                    "down": exp_down[layer].rearrange("e (p k) n -> p e (k n)", k=FF // P)}
            tiles = MOE_TILES * EXPERT_GROUPS

            def load(j, expert):
                kind = ("gate", "up", "down")[j // 4]
                sp.dma_start(moe_slot(j).rearrange("p (e c) -> p e c", e=PER_GROUP),
                             rows[kind][:, bass.ds(expert, PER_GROUP),
                                        (j % 4) * 1024:(j % 4 + 1) * 1024]).then_inc(s_ring[MOE_SLOT[j]], 16)

            for j in range(MOE_TILES):
                at = MOE_SLOT[j]
                if at in MOE_SLOT[:j]:
                    sp.wait_ge(s_used, first + last_user(j) + 1)
                elif at in (6, 7):
                    free_work_slots(sp, layer, at)
                elif at < DENSE_RING:
                    sp.wait_ge(s_used, first - DENSE_RING + at + 1)
                else:
                    sp.wait_ge(s_used, first)
                load(j, 0)
            with sp.Fori(1, EXPERT_GROUPS) as it:
                for j in range(MOE_TILES):
                    sp.wait_ge(s_used, it * MOE_TILES + (first + last_user(j) + 1))
                    load(j, it * PER_GROUP)
            sp.wait_ge(m[layer]["slots_ready"], 1)
            count = overflow_blocks(sp, layer)
            o = m[layer]["over"]
            with sp.If(count > 0):
                sp.wait_ge(s_used, first + tiles)
                with sp.Fori(0, count) as b:
                    e = sp.value_load(blocks[0:1, bass.ds(b, 1)], min_val=0, max_val=NE - 1)
                    for j, kind in enumerate(("gate", "up", "down")):
                        sp.wait_ge(o["used"], 3 * b + 1)
                        sp.dma_start(ring[:, j, :].rearrange("p (e c) -> p e c", e=1),
                                     rows[kind][:, bass.ds(e, 1), :]).then_inc(o[f"loaded{j}"], 16)
            return count

        def route_pe(pe, layer):
            s = m[layer]
            i = 1 + 2 * layer
            pe.wait_ge(s["route_w"], 16 * 4)
            for b in range(KD // 2):
                pe.wait_ge(s_xT_act if b % 2 == 0 else s_xT_dve, batches_done(i, b, False))
                for k in (2 * b, 2 * b + 1):
                    for t in range(TT):
                        last = nc.tensor.matmul(bank[2 + t][:, 0:36], xT[:, k, t * P:(t + 1) * P],
                                                w_route[:, k, :], start=(k == 0), stop=(k == KD - 1))
            last.then_inc(s["logits"], 1)
            pe.wait_ge(s["chosen"], 1)
            A = rt[:, 0:64].rearrange("p (t e) -> p t e", t=TT)
            nc.tensor.matmul(bank[4][:, 0:32], tri, A[:, 0, :], start=True, stop=True)
            nc.tensor.matmul(bank[4][:, 32:64], ones, A[:, 0, :], start=True, stop=False)
            nc.tensor.matmul(bank[4][:, 32:64], tri, A[:, 1, :], start=False, stop=True).then_inc(s["ranked"], 1)
            nc.tensor.matmul(bank[5][:, 0:32], ones, A[:, 0, :], start=True,
                             stop=False).then_inc(s["over"]["used"], 1)
            nc.tensor.matmul(bank[5][:, 0:32], ones, A[:, 1, :], start=False, stop=True).then_inc(s["ranked"], 1)

        def route_act(act, layer):
            s = m[layer]
            act.wait_ge(s["exp_in"], 1)
            nc.scalar.activation(m_t[:, 0, 0:8], m_t[:, 0, 0:8], ACT.Exp).then_inc(s["exp_out"], 1)
            act.wait_ge(s["top_in"], 1)
            nc.scalar.activation(m_t[:, 1, 0:2], m_t[:, 1, 0:2], ACT.Exp).then_inc(s["top_out"], 1)

        def route_dve(dve, layer, first_sel):
            s = m[layer]
            chain = Chain(dve, s["step"])
            V = nc.vector
            A = rt[:, 0:64].rearrange("p (t e) -> p t e", t=TT)
            at = [0]
            scratch = xT2[:, :, :].rearrange("p k s -> p (k s)")

            def tmp(*shape):
                size = int(np.prod(shape))
                v = scratch[:, at[0]:at[0] + size]
                at[0] += size
                return v.rearrange("p (a b) -> p a b", b=shape[1]) if len(shape) == 2 else v

            def over_last(v, n):
                return v.unsqueeze(2).to_broadcast([P, TT, n])

            def over_tiles(v, n):
                return v.unsqueeze(1).to_broadcast([P, TT, n])

            own = tmp(NE)
            chain(V.tensor_scalar(own, iota[:, 0:NE], float(SLOTS), None, ALU.mult))
            L = tmp(TT, 36)
            dve.wait_ge(s["logits"], 1)
            dve.wait_ge(s["route_w"], 16 * 4)
            chain(V.tensor_tensor(L, pair[:, :].rearrange("p (t c) -> p t c", t=TT)[:, :, 0:36],
                                  over_tiles(b_route[:], 36), ALU.add))

            def first_max(scores, n):
                top, low = tmp(TT), tmp(TT)
                place, hot = tmp(TT, n), tmp(TT, n)
                chain(V.tensor_reduce(top, scores, AX, ALU.max))
                chain(V.tensor_tensor(place, scores, over_last(top, n), ALU.is_ge))
                chain(V.scalar_tensor_tensor(out=place, in0=place, scalar=-99.0, in1=over_tiles(iota[:, 0:n], n),
                                             op0=ALU.mult, op1=ALU.add))
                chain(V.tensor_reduce(low, place, AX, ALU.min))
                chain(V.tensor_tensor(hot, place, over_last(low, n), ALU.is_equal))
                return top, hot

            gtop, ghot = first_max(L[:, :, 0:MG], MG)
            V.tensor_tensor(m_t[:, 0, 0:8].rearrange("p (t g) -> p t g", t=TT), L[:, :, 0:MG],
                            over_last(gtop, MG), ALU.subtract).then_inc(s["exp_in"], 1)
            pen = tmp(TT, MG)
            chain(V.tensor_scalar(pen, ghot, FAR, -FAR, ALU.mult, ALU.add))
            E1 = tmp(TT, NE)
            for t in range(TT):
                last = V.tensor_tensor(E1[:, t, :].rearrange("p (g e) -> p g e", g=MG),
                                       L[:, t, MG:].rearrange("p (g e) -> p g e", g=MG),
                                       pen[:, t, :].unsqueeze(2).to_broadcast([P, MG, EPG]), ALU.add)
                chain(last)
            top1, hot1 = first_max(E1, NE)
            E2 = tmp(TT, NE)
            chain(V.scalar_tensor_tensor(out=E2, in0=hot1, scalar=-2.0 * FAR, in1=E1, op0=ALU.mult, op1=ALU.add))
            top2, hot2 = first_max(E2, NE)
            V.tensor_tensor(A, hot1, hot2, ALU.add).then_inc(s["chosen"], 1)
            V.tensor_tensor(m_t[:, 1, 0:2], top2, top1, ALU.subtract).then_inc(s["top_in"], 1)
            psum, r = tmp(TT), tmp(TT)
            dve.wait_ge(s["exp_out"], 1)
            chain(V.tensor_reduce(psum, m_t[:, 0, 0:8].rearrange("p (t g) -> p t g", t=TT), AX, ALU.add))
            dve.wait_ge(s["top_out"], 1)
            chain(V.tensor_scalar(r, m_t[:, 1, 0:2], 1.0, None, ALU.add))
            chain(V.tensor_tensor(r, r, psum, ALU.mult))
            chain(V.reciprocal(gate_of[:, 0, :], r))
            chain(V.tensor_tensor(gate_of[:, 1, :], gate_of[:, 0, :], m_t[:, 1, 0:2], ALU.mult))
            far, slots = tmp(TT, NE), tmp(TT, NE)
            mine = [tmp(TT, NE), tmp(TT, NE)]

            def choose_slots():
                for i, hot in enumerate((hot1, hot2)):
                    last = V.tensor_tensor(mine[i], hot, slots, ALU.mult)
                chain(last)
                for i in range(2):
                    last = V.tensor_reduce(slot_of[:, i, :], mine[i], AX, ALU.add)
                chain(last)

            ranks = bank[4][:, 0:64].rearrange("p (t e) -> p t e", t=TT)
            dve.wait_ge(s["ranked"], 1)
            V.tensor_scalar(far, ranks, float(SLOTS), float(2 * NE * SLOTS), ALU.is_ge, ALU.mult)
            chain(V.tensor_tensor(slots, ranks, over_tiles(own, NE), ALU.add))
            chain(V.tensor_tensor(slots, slots, far, ALU.add))
            choose_slots()
            first_sel()
            more = tmp(NE)
            dve.wait_ge(s["ranked"], 2)
            counts = bank[5][:, 0:32]
            chain(V.tensor_scalar(more, counts, float(SLOTS), None, ALU.is_gt))
            for r_ in range(2, S // SLOTS):
                chain(V.scalar_tensor_tensor(out=more, in0=counts, scalar=float(SLOTS * r_), in1=more,
                                             op0=ALU.is_gt, op1=ALU.add))
            ends, step = more, 1
            while step < NE:
                new = tmp(NE)
                V.tensor_copy(new[:, 0:step], ends[:, 0:step])
                chain(V.tensor_tensor(new[:, step:NE], ends[:, step:NE], ends[:, 0:NE - step], ALU.add))
                ends, step = new, 2 * step
            shift = tmp(NE)
            chain(V.tensor_tensor(shift, ends, more, ALU.subtract))
            chain(V.scalar_tensor_tensor(out=shift, in0=shift, scalar=float(SLOTS), in1=own,
                                         op0=ALU.mult, op1=ALU.subtract))
            chain(V.tensor_scalar(shift, shift, float(NE * SLOTS - SLOTS), None, ALU.add))
            chain(V.scalar_tensor_tensor(out=slots, in0=ranks, scalar=float(SLOTS), in1=over_tiles(shift, NE),
                                         op0=ALU.is_ge, op1=ALU.mult))
            chain(V.tensor_tensor(slots, slots, ranks, ALU.add))
            chain(V.tensor_tensor(slots, slots, over_tiles(own, NE), ALU.add))
            choose_slots()
            whose, expert = tmp(MAX_OVERFLOW, NE), tmp(MAX_OVERFLOW)
            chain(V.tensor_tensor(whose[0:1], ends[0:1].unsqueeze(1).to_broadcast([1, MAX_OVERFLOW, NE]),
                                  iota[0:1, 0:MAX_OVERFLOW].unsqueeze(2).to_broadcast([1, MAX_OVERFLOW, NE]),
                                  ALU.is_le))
            chain(V.tensor_reduce(expert[0:1], whose[0:1], AX, ALU.add))
            chain(V.tensor_scalar(expert[0:1], expert[0:1], float(NE - 1), None, ALU.min))
            V.tensor_copy(blocks[0:1, MAX_OVERFLOW:MAX_OVERFLOW + 1],
                          ends[0:1, NE - 1:NE]).then_inc(s["over"]["h_added"], 1)
            dve.wait_ge(s["over"]["h_added"], 1)
            V.tensor_copy(blocks[0:1, 0:MAX_OVERFLOW], expert[0:1]).then_inc(s["slots_ready"], 1)
            dve.wait_ge(s["slots_ready"], 1)

        def group_pe(pe, layer, it, experts, s, over):
            first = FIRST_MOE[layer]
            M = experts * SLOTS
            pe.wait_ge(s["sel_ready"], 2 * it + 1)
            if over:
                pe.wait_ge(s["h_added"], 4 * it + 1)
                pe.wait_ge(s_h, MOE_H0[layer] + 4 * EXPERT_GROUPS)
            else:
                pe.wait_ge(s_h, MOE_H0[layer] + 4 * it)
            for b in range(2):
                for kk in range(4):
                    for t in range(TT):
                        last = nc.tensor.matmul(bank[b][:, kk * M:(kk + 1) * M], hn[:, t, 4 * b + kk::KD],
                                                m_sel[:, t, 0:M], start=(t == 0), stop=(t == TT - 1))
                last.then_inc(s["gathered"], 1)
            pe.wait_ge(s["sel_ready"], 2 * it + 2)
            for t in range(TT):
                last = nc.tensor.transpose(bank[6][0:M, t * P:(t + 1) * P], m_gsel[:, t, 0:M], ident)
            last.then_inc(s["gselT_done"], 1)
            pe.wait_ge(s["x_ready"], 2 * it + 2)

            def used(last, j):
                if not over:
                    last.then_inc(s_used, 1)
                elif j % 4 == 3:
                    last.then_inc(s["used"], 1)

            def weights(j):
                if not over:
                    at = MOE_SLOT[j]
                    loads = loads_before(layer, at) + MOE_SLOT[:j].count(at) + 1
                    pe.wait_ge(s_ring[at], it * (16 * MOE_SLOT.count(at)) + 16 * loads)
                    return moe_slot(j).rearrange("p (e c) -> p e c", e=experts)
                if j % 4 == 0:
                    pe.wait_ge(s[f"loaded{j // 4}"], 16 * it + 16)
                return ring[:, j // 4, (j % 4) * 1024:(j % 4 + 1) * 1024].unsqueeze(1)

            for kind in range(2):
                for c in range(4):
                    w = weights(4 * kind + c)
                    for kk in range(2):
                        k = 2 * c + kk
                        for e in range(experts):
                            rows = slice(e * SLOTS, (e + 1) * SLOTS)
                            last = nc.tensor.matmul(bank[2 + kind][rows, :], m_x[:, k, rows],
                                                    w[:, e, kk * FF:(kk + 1) * FF],
                                                    start=(k == 0), stop=(k == KD - 1))
                    used(last, 4 * kind + c)
            pe.wait_ge(s["hid_ready"], it + 1)
            for k in range(4):
                last = nc.tensor.transpose(bank[7][:, k * P:(k + 1) * P], m_hid[:, k::4], ident)
            last.then_inc(s["hidT_done"], 1)
            pe.wait_ge(s["hidT_ready"], it + 1)
            for k in range(4):
                w = weights(8 + k)
                for nh in range(2):
                    for e in range(experts):
                        rows = slice(e * SLOTS, (e + 1) * SLOTS)
                        last = nc.tensor.matmul(bank[4 + nh][rows, :],
                                                m_hidT[:, k * P + e * SLOTS:k * P + (e + 1) * SLOTS],
                                                w[:, e, nh * 512:(nh + 1) * 512], start=(k == 0), stop=(k == 3))
                    if k == 3 and nh == 0:
                        last.then_inc(s["y_done"], 1)
                used(last, 8 + k)
            pe.wait_ge(s["gselT_ready"], it + 1)
            for nh in range(2):
                pe.wait_ge(s["y_ready"], 2 * it + nh + 1)
                for t in range(TT):
                    i = 2 * nh + t
                    if i >= 2:
                        if over:
                            pe.wait_ge(s["h_added"], 4 * it + i)
                        else:
                            pe.wait_ge(s_h, MOE_H0[layer] + 4 * it + i - 1)
                    nc.tensor.matmul(bank[t], m_gselT[0:M, t * P:(t + 1) * P], m_y[0:M, nh * 512:(nh + 1) * 512],
                                     start=True, stop=True).then_inc(s["combined"], 1)

        def group_act(act, layer, it, experts, s, over):
            first = FIRST_MOE[layer]
            M = experts * SLOTS

            def tiles_done(j):
                if over:
                    act.wait_ge(s["used"], 3 * it + j // 4 + 1)
                else:
                    act.wait_ge(s_used, it * MOE_TILES + first + j)

            for b in range(2):
                act.wait_ge(s["gathered"], 2 * it + b + 1)
                for kk in range(4):
                    k = 4 * b + kk
                    last = nc.scalar.mul(m_x[:, k, 0:M], bank[b][:, kk * M:(kk + 1) * M],
                                         gains[:, 1 + 2 * layer, k:k + 1])
                last.then_inc(s["x_ready"], 1)
            act.wait_ge(s["gselT_done"], it + 1)
            if over:
                act.wait_ge(s["h_added"], 4 * it + 1)
            else:
                act.wait_ge(s_h, MOE_H0[layer] + 4 * it)
            nc.scalar.copy(m_gselT[0:M, :], bank[6][0:M, 0:S]).then_inc(s["gselT_ready"], 1)
            tiles_done(4)
            nc.scalar.activation(m_sg[0:M, :], bank[2][0:M, :], ACT.Silu).then_inc(s["silu_ready"], 1)
            act.wait_ge(s["hidT_done"], it + 1)
            nc.scalar.copy(m_hidT[:, :], bank[7]).then_inc(s["hidT_ready"], 1)
            act.wait_ge(s["y_done"], it + 1)
            nc.scalar.copy(m_y[0:M, 0:512], bank[4][0:M, :]).then_inc(s["y_ready"], 1)
            tiles_done(12)
            nc.scalar.copy(m_y[0:M, 512:1024], bank[5][0:M, :]).then_inc(s["y_ready"], 1)

        def next_slots(dve, chain, M):
            nc.vector.tensor_scalar(slot_of[:, 0, :], slot_of[:, 0, :], -float(M), None, ALU.add)
            chain(nc.vector.tensor_scalar(slot_of[:, 1, :], slot_of[:, 1, :], -float(M), None, ALU.add))

        def select(dve, n, M, s):
            V = nc.vector
            chain = Chain(dve, s["dve"], n * DVE_PER_GROUP)
            for t in range(TT):
                V.tensor_scalar(m_t[:, t, 0:M], iota[:, 0:M], slot_of[:, 1, t:t + 1], None, ALU.is_equal)
                last = V.tensor_scalar(m_gsel[:, t, 0:M], iota[:, 0:M], slot_of[:, 0, t:t + 1], None, ALU.is_equal)
            chain(last)
            for t in range(TT):
                last = V.tensor_tensor(m_sel[:, t, 0:M], m_t[:, t, 0:M], m_gsel[:, t, 0:M], ALU.add)
            last.then_inc(s["sel_ready"], 1)
            for t in range(TT):
                last = V.tensor_scalar(m_gsel[:, t, 0:M], m_gsel[:, t, 0:M], gate_of[:, 0, t:t + 1], None,
                                       ALU.mult)
            chain(last)
            for t in range(TT):
                last = V.scalar_tensor_tensor(out=m_gsel[:, t, 0:M], in0=m_t[:, t, 0:M],
                                              scalar=gate_of[:, 1, t:t + 1], in1=m_gsel[:, t, 0:M],
                                              op0=ALU.mult, op1=ALU.add)
            last.then_inc(s["sel_ready"], 1)

        def group_dve(dve, layer, it, experts, s, over):
            first = FIRST_MOE[layer]
            M = experts * SLOTS
            V = nc.vector
            chain = Chain(dve, s["dve"], it * DVE_PER_GROUP + 2)
            if over:
                select(dve, it, M, s)
            dve.wait_ge(s["silu_ready"], it + 1)
            if over:
                dve.wait_ge(s["used"], 3 * it + 3)
            else:
                dve.wait_ge(s_used, it * MOE_TILES + first + 8)
            V.tensor_tensor(m_hid[0:M, :], m_sg[0:M, :], bank[3][0:M, :], ALU.mult).then_inc(s["hid_ready"], 1)
            if not over:
                next_slots(dve, chain, M)
                dve.wait_ge(s["gselT_done"], it + 1)
                select(dve, it + 1, M, s)
            for i in range(4):
                nh, t = i // 2, i % 2
                dve.wait_ge(s["combined"], 4 * it + i + 1)
                hs = h[:, t, nh * 512:(nh + 1) * 512]
                V.tensor_tensor(hs, hs, bank[t], ALU.add).then_inc(s["h_added"] if over else s_h, 1)
            if over:
                next_slots(dve, chain, M)

        def moe_engine(engine, layer, group):
            with engine.Fori(0, EXPERT_GROUPS) as it:
                group(engine, layer, it, PER_GROUP, m[layer]["main"], False)
            engine.wait_ge(m[layer]["slots_ready"], 1)
            count = overflow_blocks(engine, layer)
            with engine.If(count > 0):
                with engine.Fori(0, count) as b:
                    group(engine, layer, b, 1, m[layer]["over"], True)

        def overflow_blocks(engine, layer):
            return engine.value_load(blocks[0:1, MAX_OVERFLOW:MAX_OVERFLOW + 1], min_val=0,
                                     max_val=MAX_OVERFLOW)

        PAIRS = GROUPS * DIL_H // 2
        DEPTH_DEN = 4
        d_q = area(0, PAIRS, S)
        d_k = area(PAIRS * S, PAIRS, S)
        d_v = area(2 * PAIRS * S, TT, QCOLS)
        flat_x = xT[:, :, :].rearrange("p k s -> p (k s)")
        flat_x2 = xT2[:, :, :].rearrange("p k s -> p (k s)")
        flat_hn = hn[:, :, :].rearrange("p t d -> p (t d)")
        d_raw = [flat_hn[:, i * 512:(i + 1) * 512] for i in range(2)]
        d_nrm = [flat_hn[:, 1024 + i * 512:1024 + (i + 1) * 512] for i in range(2)]
        d_sq = rt[:, 0:512]
        d_ss = sb("head_squares", [P, 2, 8])
        d_sd = sb("head_std", [P, 2, 8])
        d_bias = [flat_x[:, i * GROUPS * S:(i + 1) * GROUPS * S].rearrange("p (g n) -> p g n", g=GROUPS)
                  for i in range(2)]
        W0, W1 = GROUPS * P, GROUPS * S
        d_p = [f[:, 0:W0 + W1] for f in (flat_x2, flat_hn)]
        d_spare = sb("pT_piece", [P, W0])
        d_pT = [[flat_x2[:, W0 + W1:2 * W0 + W1], flat_x2[:, 2 * W0 + W1:3 * W0 + W1], d_spare[:]],
                [flat_hn[:, W0 + W1:2 * W0 + W1], flat_hn[:, 2 * W0 + W1:3 * W0 + W1],
                 flat_x[:, 2 * W1:2 * W1 + W0]]]
        d_max = sb("row_max", [P, 2, TT])
        d_neg = sb("row_max_negated", [P, 2, TT])
        d_den = sb("row_sum", [P, DEPTH_DEN, TT])
        d_inv = sb("row_sum_inverse", [P, 2, TT])
        bias_tab = work[:, 12288:12288 + BW]
        bias_mask = work[:, 12288 + BW:12288 + 2 * BW]
        bias_rel = work[:, 12288 + 2 * BW:12288 + 2 * BW + GROUPS * DIL_H]
        bias_out = work[:, 13500:13500 + BW]

        s_btab = sem("bias_tables_loaded")
        b_done = sem("bias_rows_made")
        b_kept = sem("bias_rows_kept")
        b_stored = sem("bias_rows_stored")
        b_loaded = [sem(f"bias_loaded{i}") for i in range(2)]
        s_qkg = sem("qk_gain_loaded")
        q_done = sem("dil_tile_projected")
        q_raw = sem("dil_raw_kept")
        q_sq = sem("dil_squared")
        q_var = sem("dil_variance")
        q_std = sem("dil_std")
        q_nrm = sem("dil_normed")
        q_tp = sem("dil_transposed")
        q_kept = sem("dil_qk_kept")
        v_act = sem("dil_v_by_act")
        v_dve = sem("dil_v_by_dve")
        a_sc = sem("att_scores")
        a_sum = sem("att_biased")
        a_neg = sem("att_max_ready")
        a_exp = sem("att_exp")
        a_tp = sem("att_transposed")
        a_pT_act = sem("att_pT_by_act")
        a_pT_dve = sem("att_pT_by_dve")
        a_o = sem("att_out")
        a_kept = sem("att_out_kept")
        a_turned = sem("att_out_transposed")
        a_aT_act = sem("att_aT_by_act")
        a_aT_dve = sem("att_aT_by_dve")
        a_proj = sem("att_projected")

        def bias_pe(pe):
            pe.wait_ge(s_btab, 16 * 3)
            nc.tensor.matmul(bank[7][0:GROUPS * DIL_H, 0:BW], bias_rel[0:BUCKETS, :], bias_tab[0:BUCKETS, :],
                             start=True, stop=True).then_inc(b_done, 1)

        def bias_dve(dve):
            dve.wait_ge(b_done, 1)
            nc.vector.tensor_tensor(bias_out[0:GROUPS * DIL_H, :], bank[7][0:GROUPS * DIL_H, 0:BW],
                                    bias_mask[0:GROUPS * DIL_H, :], ALU.add).then_inc(b_kept, 1)

        UNITS = 2 * 2 * N_KV
        LAST_B = FIRST_QKV + DENSE_B - 1

        def dilated_pe(pe):
            xT_ready(pe, 2)

            def turn(u):
                pe.wait_ge(q_nrm, u + 1)
                if u >= 2:
                    pe.wait_ge(q_kept, u - 1)
                for b in range(4):
                    last = nc.tensor.transpose(bank[u % 2][:, b * P:(b + 1) * P],
                                               d_nrm[u % 2][:, b * P:(b + 1) * P], ident)
                last.then_inc(q_tp, 1)

            for i in range(2 * N_KV):
                src = (xq_hi, xq_lo) if i < N_KV else (x_hi, x_lo)
                for t in range(TT):
                    u = 2 * i + t
                    if u >= 4:
                        pe.wait_ge(q_raw, u - 3)
                    last = project(pe, bank[2 + u % 4], src, FIRST_QKV + i, t)
                    if t == 0:
                        last.then_inc(q_done, 1)
                    else:
                        last.then_inc(s_used, 1)
                    if u >= 1:
                        turn(u - 1)
            for i in range(N_KV):
                n = FIRST_QKV + 2 * N_KV + i
                for t in range(TT):
                    if i >= 2:
                        pe.wait_ge((v_act, v_dve)[t], i - 1)
                    elif i == 0 and t == 0:
                        pe.wait_ge(q_raw, UNITS)
                    last = project(pe, bank[2 + 2 * (i % 2) + t], (x_hi, x_lo), n, t)
                    if t == 0:
                        last.then_inc(q_done, 1)
                last.then_inc(s_used, 1)
                if i == 0:
                    turn(UNITS - 1)
            pe.wait_ge(q_kept, UNITS)
            pe.wait_ge(v_act, N_KV)
            pe.wait_ge(v_dve, N_KV)
            for i in range(DIL_H + 2):
                if i < DIL_H:
                    if i >= 1:
                        pe.wait_ge(a_sum, 2 * i)
                    rows = slice((i % 2) * DIL_DH, (i % 2 + 1) * DIL_DH)
                    for g in range(GROUPS):
                        pr = g * DIL_H // 2 + i // 2
                        last = nc.tensor.matmul(bank[0][:, g * P:(g + 1) * P], d_q[rows, pr, 0:P],
                                                d_k[rows, pr, 0:P], start=True, stop=True)
                    last.then_inc(a_sc, 1)
                    for g in range(GROUPS):
                        pr = g * DIL_H // 2 + i // 2
                        last = nc.tensor.matmul(pair[:, g * S:(g + 1) * S], d_q[rows, pr, P:S],
                                                d_k[rows, pr, :], start=True, stop=True)
                    last.then_inc(a_sc, 1)
                if 1 <= i <= DIL_H:
                    hd = i - 1
                    for b in range(3):
                        if b < 2:
                            pe.wait_ge(a_exp, 2 * hd + b + 1)
                        if hd >= 1 and b < 2:
                            pe.wait_ge((a_pT_act, a_pT_dve)[b], 2 * hd - 1 if b == 0 else hd)
                        elif hd >= 1:
                            pe.wait_ge(a_pT_act, 2 * hd)
                        for j in range(3):
                            c = (3 * b + j) * P
                            last = nc.tensor.transpose(bank[4 + b][:, j * P:(j + 1) * P],
                                                       d_p[hd % 2][:, c:c + P], ident)
                        last.then_inc(a_tp, 1)
                if i >= 2:
                    hd = i - 2
                    pe.wait_ge(a_pT_act, 2 * hd + 2)
                    pe.wait_ge(a_pT_dve, hd + 1)
                    if hd >= 2:
                        pe.wait_ge(a_kept, hd - 1)
                    o = bank[1 if hd % 2 == 0 else 7]
                    pT = d_pT[hd % 2]
                    for g in range(GROUPS):
                        cols = slice(g * D + hd * DIL_DH, g * D + (hd + 1) * DIL_DH)
                        nc.tensor.matmul(o[:, 0:DIL_DH], pT[0][:, g * P:(g + 1) * P], d_v[:, 0, cols],
                                         start=(g == 0), stop=(g == GROUPS - 1))
                    for j in range(2 * GROUPS):
                        g, kt = j // 2, j % 2
                        cols = slice(g * D + hd * DIL_DH, g * D + (hd + 1) * DIL_DH)
                        last = nc.tensor.matmul(o[:, DIL_DH:2 * DIL_DH],
                                                pT[1 + j // 3][:, (j % 3) * P:(j % 3 + 1) * P],
                                                d_v[:, kt, cols], start=(j == 0), stop=(j == 2 * GROUPS - 1))
                    last.then_inc(a_o, 1)
            pe.wait_ge(a_kept, DIL_H)
            for b in range(KD // 2):
                if b >= 2:
                    pe.wait_ge(a_aT_dve, b - 1)
                for kk in range(2):
                    for t in range(TT):
                        col = (kk * TT + t) * P
                        last = nc.tensor.transpose(bank[4 + b % 2][:, col:col + P],
                                                   d_v[:, t, 2 * b + kk:D:KD], ident)
                last.then_inc(a_turned, 1)
            pe.wait_ge(a_aT_dve, KD // 2)
            project_out(pe, FIRST_WO, N_WO, 4, (aT_hi, aT_lo), a_proj)

        def dilated_act(act):
            act.wait_ge(s_qkg, 16 * 4)

            def keep(u):
                act.wait_ge(q_tp, u + 1)
                i, t = u // 2, u % 2
                j = i % N_KV
                src = bank[u % 2].rearrange("p (a s) -> p a s", a=4)
                nc.scalar.mul((d_q if i < N_KV else d_k)[:, 4 * j:4 * j + 4, t * P:(t + 1) * P],
                              backwards(src) if i < N_KV else src,
                              qk_gain[:, 1 - i // N_KV, j // 2:j // 2 + 1]).then_inc(q_kept, 1)

            for n in range(FIRST_QKV - 2, FIRST_QKV):
                split_next(split_act, act, n, LAST_B)
            for u in range(UNITS):
                i, t = u // 2, u % 2
                if t == 0:
                    act.wait_ge(q_done, i + 1)
                else:
                    act.wait_ge(s_used, FIRST_QKV + i + 1)
                if u >= 2:
                    act.wait_ge(q_nrm, u - 1)
                nc.scalar.copy(d_raw[u % 2], bank[2 + u % 4]).then_inc(q_raw, 1)
                act.wait_ge(q_raw, u + 1)
                nc.scalar.activation(d_sq, d_raw[u % 2], ACT.Square).then_inc(q_sq, 1)
                if u >= 1:
                    keep(u - 1)
                act.wait_ge(q_var, u + 1)
                nc.scalar.activation(d_sd[:, u % 2, :], d_ss[:, u % 2, :], ACT.Sqrt).then_inc(q_std, 1)
                if t == 1:
                    split_next(split_act, act, FIRST_QKV + i, LAST_B)
            for i in range(N_KV):
                act.wait_ge(q_done, 2 * N_KV + i + 1)
                nc.scalar.copy(d_v[:, 0, i * 512:(i + 1) * 512], bank[2 + 2 * (i % 2)]).then_inc(v_act, 1)
                if i == 0:
                    keep(UNITS - 1)
                split_next(split_act, act, FIRST_QKV + 2 * N_KV + i, LAST_B)
            for i in range(DIL_H + 1):
                if i < DIL_H:
                    act.wait_ge(a_neg, i + 1)
                    for t in range(TT):
                        p = d_p[i % 2][:, 0:W0] if t == 0 else d_p[i % 2][:, W0:W0 + W1]
                        nc.scalar.activation(p, p, ACT.Exp, bias=d_neg[:, i % 2, t:t + 1],
                                             accum_out=d_den[:, i % DEPTH_DEN, t:t + 1]).then_inc(a_exp, 1)
                if i >= 1:
                    hd = i - 1
                    if hd >= 2:
                        act.wait_ge(a_o, hd - 1)
                    for b in (0, 2):
                        act.wait_ge(a_tp, 3 * hd + b + 1)
                        nc.scalar.copy(d_pT[hd % 2][b], bank[4 + b][:, 0:W0]).then_inc(a_pT_act, 1)
            for b in range(KD // 2):
                act.wait_ge(a_turned, b + 1)
                nc.scalar.copy(aT_hi[:, 2 * b:2 * b + 2, :].rearrange("p k (t s) -> p (k t) s", t=TT),
                               backwards(bank[4 + b % 2].rearrange("p (a s) -> p a s", a=4))
                               ).then_inc(a_aT_act, 1)

        def dilated_dve(dve, chain):
            for n in range(FIRST_QKV - 2, FIRST_QKV):
                split_next(split_dve, dve, n, LAST_B)
            for u in range(UNITS):
                dve.wait_ge(q_sq, u + 1)
                ss = d_ss[:, u % 2, :]
                chain(nc.vector.tensor_reduce(ss, d_sq.rearrange("p (h d) -> p h d", d=DIL_DH), AX, ALU.add))
                nc.vector.tensor_scalar(ss, ss, 1.0 / DIL_DH, EPS, ALU.mult, ALU.add).then_inc(q_var, 1)
                dve.wait_ge(q_std, u + 1)
                sd = d_sd[:, u % 2, :]
                chain(nc.vector.reciprocal(sd, sd))
                if u >= 2:
                    dve.wait_ge(q_tp, u - 1)
                scale = DIL_DH ** -0.5 if u < UNITS // 2 else 1.0
                nc.vector.scalar_tensor_tensor(
                    out=d_nrm[u % 2].rearrange("p (h d) -> p h d", d=DIL_DH),
                    in0=d_raw[u % 2].rearrange("p (h d) -> p h d", d=DIL_DH), scalar=scale,
                    in1=sd.unsqueeze(2).to_broadcast([P, 8, DIL_DH]),
                    op0=ALU.mult, op1=ALU.mult).then_inc(q_nrm, 1)
                if u % 2 == 1:
                    split_next(split_dve, dve, FIRST_QKV + u // 2, LAST_B)
            for i in range(N_KV):
                dve.wait_ge(s_used, FIRST_QKV + 2 * N_KV + i + 1)
                nc.vector.tensor_copy(d_v[:, 1, i * 512:(i + 1) * 512],
                                      bank[3 + 2 * (i % 2)]).then_inc(v_dve, 1)
                split_next(split_dve, dve, FIRST_QKV + 2 * N_KV + i, LAST_B)
            for i in range(DIL_H + 2):
                if i < DIL_H:
                    dve.wait_ge(b_loaded[i % 2], 16 * (i // 2 + 1))
                    if i >= 2:
                        dve.wait_ge(a_tp, 3 * (i - 1))
                    else:
                        dve.wait_ge(q_tp, UNITS)
                    for t in range(TT):
                        dve.wait_ge(a_sc, 2 * i + t + 1)
                        if t == 0:
                            src, add = bank[0][:, 0:W0], d_bias[i % 2][:, :, P:S]
                            dst = d_p[i % 2][:, 0:W0]
                        else:
                            src, add = pair[:, 0:W1], d_bias[i % 2]
                            dst = d_p[i % 2][:, W0:W0 + W1]
                        three = "p (g n) -> p g n"
                        nc.vector.tensor_tensor_reduce(
                            out=dst.rearrange(three, g=GROUPS), in0=src.rearrange(three, g=GROUPS), in1=add,
                            scale=1.0, scalar=-3.0e38, op0=ALU.add, op1=ALU.max,
                            accum_out=d_max[:, i % 2, t:t + 1]).then_inc(a_sum, 1)
                    dve.wait_ge(a_sum, 2 * i + 2)
                    nc.vector.tensor_scalar(d_neg[:, i % 2, :], d_max[:, i % 2, :], -1.0, None,
                                            ALU.mult).then_inc(a_neg, 1)
                if 1 <= i <= DIL_H:
                    hd = i - 1
                    if hd >= 2:
                        dve.wait_ge(a_o, hd - 1)
                    dve.wait_ge(a_tp, 3 * hd + 2)
                    nc.vector.tensor_copy(d_pT[hd % 2][1], bank[5][:, 0:W0]).then_inc(a_pT_dve, 1)
                if i >= 2:
                    hd = i - 2
                    dve.wait_ge(a_exp, 2 * hd + 2)
                    chain(nc.vector.reciprocal(d_inv[:, hd % 2, :], d_den[:, hd % DEPTH_DEN, :]))
                    dve.wait_ge(a_o, hd + 1)
                    o = bank[1 if hd % 2 == 0 else 7][:, 0:TT * DIL_DH].rearrange("p (t d) -> p t d", t=TT)
                    nc.vector.tensor_tensor(d_v[:, :, hd * DIL_DH:(hd + 1) * DIL_DH], o,
                                            d_inv[:, hd % 2, :].unsqueeze(2).to_broadcast([P, TT, DIL_DH]),
                                            ALU.mult).then_inc(a_kept, 1)
            for b in range(KD // 2):
                dve.wait_ge(a_aT_act, b + 1)
                rows = slice(2 * b, 2 * b + 2)
                nc.vector.tensor_tensor(aT_lo[:, rows, :].rearrange("p k (t s) -> p (k t) s", t=TT),
                                        backwards(bank[4 + b % 2].rearrange("p (a s) -> p a s", a=4)),
                                        aT_hi[:, rows, :].bitcast(F32).rearrange("p k (t s) -> p (k t) s", t=TT),
                                        ALU.subtract).then_inc(a_aT_dve, 1)
            add_out_dve(dve, FIRST_WO, N_WO, a_proj)

        block = ctx.enter_context(nc.Block())

        @block.sync
        def _(sp):
            sp.dma_start(h[:, :, :], x[0].rearrange("(t p) d -> p t d", p=P)).then_inc(s_x, 16)
            sp.dma_start(kept[:, :], constants[:, 0:C_KEPT]).then_inc(s_small, 16)
            sp.dma_start(gains[:, 0:4:2, :], mixer_norm.rearrange("l (p k) -> p l k", k=KD)).then_inc(s_small, 16)
            sp.dma_start(gains[:, 1:4:2, :], ffn_norm.rearrange("l (p k) -> p l k", k=KD)).then_inc(s_small, 16)
            sp.dma_start(gains[:, 4, :], kv_norm.rearrange("(p k) -> p k", k=KD)).then_inc(s_small, 16)
            for i in range(N_WIN):
                load_tile(sp, FIRST_WIN + i, win[:, :, i * COLS:(i + 1) * COLS], KD)
            for i in range(N_WOUT):
                load_tile(sp, FIRST_WOUT + i, wout[:, 4 * i:4 * i + 4, :], 4)
            overflow = moe_sp(sp, 0)
            sp.wait_ge(m[0]["over"]["used"], 3 * overflow + 1)
            for i in range(3 * N_KV):
                if i < N_KV:
                    src = wq[:, :, i * COLS:(i + 1) * COLS]
                else:
                    src = wkv[:, :, (i - N_KV) * COLS:(i - N_KV + 1) * COLS]
                load_tile(sp, FIRST_QKV + i, src, KD)
            for i in range(N_WO):
                load_tile(sp, FIRST_WO + i, wo[:, 4 * i:4 * i + 4, :], 4)
            overflow = moe_sp(sp, 1)
            sp.wait_ge(s_h, H_DONE[4])
            sp.wait_ge(m[1]["over"]["h_added"], 4 * overflow + 1)
            sp.dma_start(out[0].rearrange("(t p) d -> p t d", p=P), h[:, :, :]).then_inc(s_out, 16)
            sp.wait_ge(s_out, 16)

        @block.gpsimd
        def _(pool):
            def route_loads(layer):
                s = m[layer]["route_w"]
                pool.dma_start(w_route[:, :, 0:MG], router_grp[layer].rearrange("(p k) g -> p k g", k=KD)
                               ).then_inc(s, 16)
                pool.dma_start(w_route[:, :, MG:], router_exp[layer].rearrange("(p k) e -> p k e", k=KD)
                               ).then_inc(s, 16)
                pool.dma_start(b_route[:, 0:MG], router_grp_b[layer:layer + 1, :].to_broadcast([P, MG])
                               ).then_inc(s, 16)
                pool.dma_start(b_route[:, MG:], router_exp_b[layer:layer + 1, :].to_broadcast([P, NE])
                               ).then_inc(s, 16)

            pool.dma_start(r_cos, constants[:, C_COS:C_COS + S]).then_inc(r_tab, 16)
            pool.dma_start(r_sin, constants[:, C_SIN:C_SIN + S]).then_inc(r_tab, 16)
            pool.dma_start(work[:, 16896:16896 + RET_H * DECAY_W],
                           constants[:, C_DECAY:C_DECAY + RET_H * DECAY_W]).then_inc(r_tab, 16)
            pool.dma_start(bias_tab, constants[:, C_BUCKET:C_BUCKET + BW]).then_inc(s_btab, 16)
            pool.dma_start(bias_mask, constants[:, C_MASK:C_MASK + BW]).then_inc(s_btab, 16)
            pool.dma_start(bias_rel[0:BUCKETS, :], rel_bias).then_inc(s_btab, 16)
            for half in range(2):
                rows = slice(half * DIL_DH, (half + 1) * DIL_DH)
                pool.dma_start(qk_gain[rows, 0, :], k_norm.rearrange("g d -> d g"),
                               allow_slow_non_contiguous=True).then_inc(s_qkg, 16)
                pool.dma_start(qk_gain[rows, 1, :], q_norm[0].rearrange("g d -> d g"),
                               allow_slow_non_contiguous=True).then_inc(s_qkg, 16)
            route_loads(0)
            pool.wait_ge(b_kept, 1)
            pool.dma_start(bias_rows, bias_out[0:GROUPS * DIL_H, :]).then_inc(b_stored, 16)
            pool.wait_ge(m[0]["slots_ready"], 1)
            route_loads(1)
            pool.wait_ge(b_stored, 16)
            pool.wait_ge(q_done, 3 * N_KV)
            pool.wait_ge(s_used, FIRST_WO)
            for hd in range(DIL_H):
                if hd >= 2:
                    pool.wait_ge(a_sum, 2 * (hd - 1))
                src = bass.AP(bias_rows.tensor, hd * BW, [[1, P], [DIL_H * BW, GROUPS], [1, S]])
                pool.dma_start(d_bias[hd % 2], src).then_inc(b_loaded[hd % 2], 16)

        @block.scalar
        def _(act):
            norm_act(act, 0)
            act.wait_ge(s_small, 64)
            transpose_act(act, 0, [((x_hi, x_lo), 0)])
            retention_act(act)
            norm_act(act, 1)
            transpose_act(act, 1, [(xT, 1)])
            route_act(act, 0)
            moe_engine(act, 0, group_act)
            norm_act(act, 2)
            transpose_act(act, 2, [((xq_hi, xq_lo), 2), ((x_hi, x_lo), 4)])
            dilated_act(act)
            norm_act(act, 3)
            transpose_act(act, 3, [(xT, 3)])
            route_act(act, 1)
            moe_engine(act, 1, group_act)

        @block.vector
        def _(dve):
            chain = Chain(dve, s_dv)
            norm_dve(dve, chain, 0)
            dve.wait_ge(s_small, 64)
            transpose_dve(dve, 0, [((x_hi, x_lo), 0)])
            retention_dve(dve, chain)
            norm_dve(dve, chain, 1)
            transpose_dve(dve, 1, [(xT, 1)])
            route_dve(dve, 0, lambda: select(dve, 0, PER_GROUP * SLOTS, m[0]["main"]))
            moe_engine(dve, 0, group_dve)
            norm_dve(dve, chain, 2)
            transpose_dve(dve, 2, [((xq_hi, xq_lo), 2), ((x_hi, x_lo), 4)])
            dilated_dve(dve, chain)
            norm_dve(dve, chain, 3)
            transpose_dve(dve, 3, [(xT, 3)])
            route_dve(dve, 1, lambda: select(dve, 0, PER_GROUP * SLOTS, m[1]["main"]))
            moe_engine(dve, 1, group_dve)

        @block.tensor
        def _(pe):
            pe.wait_ge(s_small, 64)
            transpose_pe(pe, 0)
            retention_pe(pe)
            transpose_pe(pe, 1)
            route_pe(pe, 0)
            moe_engine(pe, 0, group_pe)
            transpose_pe(pe, 2)
            dilated_pe(pe)
            transpose_pe(pe, 3)
            route_pe(pe, 1)
            moe_engine(pe, 1, group_pe)


_INS = ["x", "ret_w_in", "ret_w_out", "kv_norm", "w_kv", "k_norm", "dil_wq", "q_norm", "dil_wo", "rel_bias",
        "mixer_norm", "ffn_norm", "router_grp", "router_grp_b", "router_exp", "router_exp_b",
        "exp_gate", "exp_up", "exp_down"]


def kernel(**inputs):
    import numpy as _np
    import concourse.bacc as _bacc
    from concourse.bass_utils import run_bass_kernel_spmd as _run

    nc = _bacc.Bacc("TRN2", target_bir_lowering=False, num_devices=1)
    arrays, args = {}, []
    for name in _INS:
        arrays[f"in_{name}"] = _np.ascontiguousarray(inputs[name])
    arrays["shape_constants"] = shape_constants()
    for name, a in arrays.items():
        args.append(nc.dram_tensor(name, a.shape, mybir.dt.from_np(a.dtype), kind="ExternalInput").ap())
    args.append(nc.dram_tensor("out_0", (1, S, D), F32, kind="ExternalOutput").ap())
    build(nc, *args)
    r = _run(nc, [arrays], core_ids=[0])
    return r.results[0]["out_0"]
```

```python
from contextlib import ExitStack

import numpy as np

import concourse.bass as bass
from concourse import mybir

F32 = mybir.dt.float32
F32R = mybir.dt.float32r
I32 = mybir.dt.int32
ALU = mybir.AluOpType
ACT = mybir.ActivationFunctionType
AX = mybir.AxisListType.X

P = 128
D = 1024
S = 256
TT = S // P
KD = D // P
RET_H = 4
RET_DK = D // RET_H
RET_DV = 2 * RET_DK
RET_KO = RET_H * RET_DV // P
GROUPS = 3
RATES = (1, 4, 16)
WINDOWS = (128, 512, 2048)
DIL_H = 16
DIL_DH = D // DIL_H
QCOLS = GROUPS * DIL_H * DIL_DH
BUCKETS = 32
MAX_DISTANCE = 2048
MG = 4
EPG = 8
NE = MG * EPG
FF = D // 2
EPS = 1e-6
FAR = 1e30

RING = 9
FULL_RING = 6
DENSE_RING = 4
WORK = 18432
TILE = 4096
COLS = TILE // KD
SLOTS = 32
PER_GROUP = P // SLOTS
EXPERT_GROUPS = NE // PER_GROUP
MOE_TILES = 3 * 4
MAX_OVERFLOW = 16

MOE_SLOT = (6, 7, 0, 1, 2, 3, 4, 5, 8, 6, 7, 8)

N_WIN, N_WOUT, N_KV, N_WO = 12, 4, 6, 2
FIRST_WIN = 0
FIRST_WOUT = FIRST_WIN + N_WIN
FIRST_MOE = [FIRST_WOUT + N_WOUT]
FIRST_QKV = FIRST_MOE[0] + MOE_TILES * EXPERT_GROUPS
FIRST_WO = FIRST_QKV + 3 * N_KV
FIRST_MOE.append(FIRST_WO + N_WO)

DENSE_A = N_WIN + N_WOUT
DENSE_B = 3 * N_KV + N_WO

C_IDENT = 0
C_TRI = C_IDENT + P
C_ONES = C_TRI + P
C_IOTA = C_ONES + P
C_KEPT = C_IOTA + P
C_COS = C_KEPT
C_SIN = C_COS + S
C_DECAY = C_SIN + S
DECAY_W = S + P
C_BUCKET = C_DECAY + RET_H * DECAY_W
BW = 384
C_MASK = C_BUCKET + BW
C_ALL = C_MASK + BW


def shape_constants():
    c = np.zeros((P, C_ALL), np.float32)
    p = np.arange(P)
    c[:, C_IDENT:C_IDENT + P] = np.eye(P)
    c[:, C_TRI:C_TRI + P] = p[:, None] < p[None, :]
    c[:, C_ONES:C_ONES + P] = 1.0
    c[:, C_IOTA:C_IOTA + P] = p[None, :]
    half = RET_DK // 2
    inv = (1.0 / (np.float32(10000.0) ** np.linspace(0.0, 1.0, half, dtype=np.float32))).astype(np.float32)
    ang = (np.arange(S, dtype=np.float32)[None, :] * inv[:, None]).astype(np.float32)
    c[:, C_COS:C_COS + S] = np.cos(ang)
    c[:, C_SIN:C_SIN + S] = np.sin(ang)
    for h in range(RET_H):
        log_g = np.log(1.0 - 2.0 ** (-5.0 - h))
        diff = np.arange(S)[None, :] - p[:, None]
        dec = np.where(diff >= 0, np.exp(log_g * np.maximum(diff, 0)), 0.0) * RET_DK ** -0.5
        at = C_DECAY + h * DECAY_W
        c[:, at:at + S] = dec
        c[:, at + S:at + DECAY_W] = dec[:, :P]
    dist = S - 1 - np.arange(BW)
    exact = BUCKETS // 2
    n = np.maximum(dist, 0)
    nf = np.maximum(n, exact).astype(np.float32)
    large = exact + (np.log(nf / exact) / np.float32(np.log(MAX_DISTANCE / exact))
                     * (BUCKETS - exact)).astype(np.int32)
    bucket = np.where(n < exact, n, np.minimum(large, BUCKETS - 1))
    c[:BUCKETS, C_BUCKET:C_BUCKET + BW] = np.arange(BUCKETS)[:, None] == bucket[None, :]
    for g, (rate, window) in enumerate(zip(RATES, WINDOWS)):
        seen = (dist >= 0) & (dist % rate == 0) & (dist <= window)
        c[g * DIL_H:(g + 1) * DIL_H, C_MASK:C_MASK + BW] = np.where(seen, 0.0, -FAR)[None, :]
    return c


class Chain:

    def __init__(self, engine, sem, base=0):
        self.engine, self.sem, self.base, self.n = engine, sem, base, 0

    def __call__(self, instruction):
        instruction.then_inc(self.sem, 1)
        self.n += 1
        self.engine.wait_ge(self.sem, self.base + self.n)


DVE_PER_GROUP = 3


def build(nc, x, ret_w_in, ret_w_out, kv_norm, w_kv, k_norm, dil_wq, q_norm, dil_wo, rel_bias,
          mixer_norm, ffn_norm, router_grp, router_grp_b, router_exp, router_exp_b,
          exp_gate, exp_up, exp_down, constants, out):
    bias_rows = nc.dram_tensor("bias_rows", (GROUPS * DIL_H, BW), F32, kind="Internal").ap()
    ctx = ExitStack()
    with ctx:
        def sb(name, shape, dt=F32):
            return ctx.enter_context(nc.sbuf_tensor(name, shape, dt))

        def sem(name):
            return ctx.enter_context(nc.semaphore(name))

        arena_at = (nc.sbuf_base + 31) // 32 * 32
        sb("arena", [P, FULL_RING * TILE + 4 * TT * D + WORK])
        HN_AT = FULL_RING * TILE
        XT_AT = HN_AT + TT * D
        XT2_AT = XT_AT + KD * S
        H_AT = XT2_AT + KD * S
        WORK_AT = H_AT + TT * D

        def place(name, word, shape, dt=F32):
            return nc.alloc_sbuf_tensor_at(name, shape, dt, offset=arena_at + 4 * word)

        ring = place("ring", 0, [P, FULL_RING, TILE])
        ring_more = place("ring_more", WORK_AT + TILE, [P, RING - FULL_RING, TILE])
        ring_lo = place("ring_lo", 0, [P, DENSE_RING, TILE], F32R)
        ring_hi = place("ring_hi", DENSE_RING * TILE, [P, 2, TILE], F32R)
        h = place("h", H_AT, [P, TT, D])
        hn = place("hn", HN_AT, [P, TT, D])
        xT = place("xT", XT_AT, [P, KD, S])
        work = place("work", WORK_AT, [P, WORK])
        x_hi = place("x_hi", XT_AT, [P, KD, S], F32R)
        x_lo = place("x_lo", XT2_AT, [P, KD, S], F32R)
        xq_hi = place("xq_hi", WORK_AT + 12288, [P, KD, S], F32R)
        xq_lo = place("xq_lo", WORK_AT + 12288 + KD * S, [P, KD, S], F32R)
        yT_hi = place("yT_hi", WORK_AT + 12288, [P, RET_KO, S], F32R)
        yT_lo = place("yT_lo", WORK_AT, [P, RET_KO, S], F32R)
        aT_hi = place("aT_hi", WORK_AT, [P, KD, S], F32R)
        aT_lo = place("aT_lo", WORK_AT + KD * S, [P, KD, S], F32R)
        xT2 = place("xT2", XT2_AT, [P, KD, S])
        kept = sb("kept", [P, C_KEPT])
        gains = sb("gains", [P, 5, KD])
        qk_gain = sb("qk_gain", [P, 2, GROUPS])
        w_route = sb("w_route", [P, KD, MG + NE])
        b_route = sb("b_route", [P, MG + NE])
        stat = sb("stat", [P, 3, 2 * RET_H])
        root_of_no_use = sb("root_of_no_use", [P, 4])
        rt = sb("rt", [P, 512])
        slot_of = sb("slot_of", [P, 2, TT])
        gate_of = sb("gate_of", [P, 2, TT])
        blocks = sb("blocks", [P, MAX_OVERFLOW + 1], I32)
        bank = [ctx.enter_context(nc.psum_tensor(f"bank{i}", [P, 512], F32))[:, :] for i in range(2)]
        triple = ctx.enter_context(nc.psum_tensor("triple", [P, 3 * 512], F32))
        bank += [triple[:, i * 512:(i + 1) * 512] for i in range(3)]
        bank += [ctx.enter_context(nc.psum_tensor(f"bank{i}", [P, 512], F32))[:, :] for i in range(5, 8)]

        ident = kept[:, C_IDENT:C_IDENT + P]
        tri = kept[:, C_TRI:C_TRI + P]
        ones = kept[:, C_ONES:C_ONES + P]
        iota = kept[:, C_IOTA:C_IOTA + P]

        def area(at, *shape):
            size = int(np.prod(shape))
            v = work[:, at:at + size]
            if len(shape) == 2:
                return v.rearrange("p (a b) -> p a b", b=shape[1])
            if len(shape) == 3:
                return v.rearrange("p (a b c) -> p a b c", b=shape[1], c=shape[2])
            return v

        def dense_slot(n):
            return (n - (0 if n < FIRST_MOE[0] else FIRST_QKV)) % DENSE_RING

        def moe_slot(j):
            at = MOE_SLOT[j]
            return ring[:, at, :] if at < FULL_RING else ring_more[:, at - FULL_RING, :]

        def loads_before(layer, at):
            dense = (DENSE_A, DENSE_A + DENSE_B)[layer] // DENSE_RING if at < DENSE_RING else 0
            return dense + layer * MOE_SLOT.count(at) * EXPERT_GROUPS

        s_small = sem("small_loaded")
        s_x = sem("x_loaded")
        s_ring = [sem(f"ring_loaded{i}") for i in range(RING)]
        s_used = sem("ring_tiles_used")
        s_sq = sem("squares_summed")
        s_var = sem("variance_ready")
        s_std = sem("std_ready")
        s_hn = sem("hn_ready")
        s_tp = sem("transposed")
        s_xT = sem("xT_ready")
        s_dv = sem("dve_step")
        s_h = sem("h_updated")
        s_out = sem("out_stored")

        s_hi = sem("weight_halves_hi")
        s_lo = sem("weight_halves_lo")

        def load_tile(sp, n, src, parts):
            i = n if n < FIRST_MOE[0] else n - FIRST_QKV
            if i >= DENSE_RING:
                sp.wait_ge(s_used, n - DENSE_RING + 1)
            elif n >= FIRST_QKV:
                sp.wait_ge(s_used, FIRST_QKV - MOE_TILES + MOE_SLOT.index(i) + 1)
            at = dense_slot(n)
            sp.dma_start(ring[:, at, :].rearrange("p (a b) -> p a b", a=parts), src).then_inc(s_ring[at], 16)

        def dense_index(n):
            return n if n < FIRST_MOE[0] else n - FIRST_QKV + DENSE_A

        def split_act(act, n, parts=(0, 1)):
            d = dense_index(n)
            loads = dense_index(n) // DENSE_RING + 1
            if n >= FIRST_QKV:
                loads += MOE_SLOT.count(dense_slot(n)) * EXPERT_GROUPS
            if 0 in parts:
                act.wait_ge(s_ring[dense_slot(n)], 16 * loads)
                if n in (FIRST_QKV, FIRST_QKV + 1):
                    act.wait_ge(s_used, FIRST_QKV)
                elif d >= 2:
                    act.wait_ge(s_used, n - 1)
            for half in parts:
                cols = slice(half * TILE // 2, (half + 1) * TILE // 2)
                nc.scalar.copy(ring_hi[:, d % 2, cols], ring[:, dense_slot(n), cols]).then_inc(s_hi, 1)

        def split_dve(dve, n, parts=(0, 1)):
            d = dense_index(n)
            for half in parts:
                cols = slice(half * TILE // 2, (half + 1) * TILE // 2)
                dve.wait_ge(s_hi, 2 * d + half + 1)
                nc.vector.tensor_tensor(ring_lo[:, dense_slot(n), cols], ring[:, dense_slot(n), cols],
                                        ring_hi[:, d % 2, cols].bitcast(F32), ALU.subtract).then_inc(s_lo, 1)

        def split_next(split, engine, n, last):
            if n + 2 <= last:
                split(engine, n + 2)

        def halves(n, k):
            d = dense_index(n)
            return (ring_hi[:, d % 2, :].rearrange("p (k c) -> p k c", k=k),
                    ring_lo[:, dense_slot(n), :].rearrange("p (k c) -> p k c", k=k))

        def half_ready(pe, n, half):
            pe.wait_ge(s_lo, 2 * dense_index(n) + half + 1)

        def three_passes(out, left, right, first, last):
            nc.tensor.matmul(out, left[0], right[0], start=first, stop=False)
            nc.tensor.matmul(out, left[0], right[1], start=False, stop=False)
            return nc.tensor.matmul(out, left[1], right[0], start=False, stop=last)

        win = ret_w_in[0].rearrange("(p k) n -> p k n", k=KD)
        wout = ret_w_out[0].rearrange("(p k) n -> p k n", k=RET_KO)
        wkv = w_kv.rearrange("(p k) n -> p k n", k=KD)
        wq = dil_wq[0].rearrange("(p k) n -> p k n", k=KD)
        wo = dil_wo[0].rearrange("(k p) n -> p k n", p=P)


        def norm_act(act, i):
            if i == 0:
                act.wait_ge(s_x, 16)
            elif i == 2:
                act.wait_ge(s_h, H_DONE[i])
                act.wait_ge(m[0]["over"]["h_added"], 4 * overflow_blocks(act, 0) + 1)
            else:
                act.wait_ge(s_h, H_DONE[i] - 2)
            nc.scalar.activation(hn[:, 0, :], h[:, 0, :], ACT.Square, accum_out=stat[:, 0, 0:1]).then_inc(s_sq, 1)
            nc.scalar.activation(root_of_no_use[0:1, i:i + 1], h[0:1, 0, 0:1], ACT.Sqrt, scale=0.0)
            act.wait_ge(s_var, i + 1)
            nc.scalar.activation(stat[:, 2, 0:TT], stat[:, 1, 0:TT], ACT.Sqrt).then_inc(s_std, 1)

        def norm_dve(dve, chain, i):
            if i == 0:
                dve.wait_ge(s_x, 16)
            elif i == 2:
                dve.wait_ge(s_sq, TT * i + 1)
            else:
                dve.wait_ge(s_h, H_DONE[i])
            nc.vector.tensor_tensor_reduce(out=hn[:, 1, :], in0=h[:, 1, :], in1=h[:, 1, :], scale=1.0,
                                           scalar=0.0, op0=ALU.mult, op1=ALU.add,
                                           accum_out=stat[:, 0, 1:2]).then_inc(s_sq, 1)
            dve.wait_ge(s_sq, TT * (i + 1))
            nc.vector.tensor_scalar(stat[:, 1, 0:TT], stat[:, 0, 0:TT], 1.0 / D, EPS,
                                    ALU.mult, ALU.add).then_inc(s_var, 1)
            dve.wait_ge(s_std, i + 1)
            chain(nc.vector.reciprocal(stat[:, 1, 0:TT], stat[:, 2, 0:TT]))
            for t in range(TT):
                nc.vector.tensor_scalar(hn[:, t, :], h[:, t, :], stat[:, 1, t:t + 1], None,
                                        ALU.mult).then_inc(s_hn, 1)

        SPLIT_NORMS = (0, 2)
        tp_bank = (bank[0], bank[1], bank[6], bank[7])
        s_xT_act = sem("xT_batches_by_act")
        s_xT_dve = sem("xT_batches_by_dve")

        def batches_done(i, b, by_act):
            before = sum((4, 2, 8, 2)[:i])
            return before + (b + 1 if i in SPLIT_NORMS else b // 2 + 1)

        def transpose_pe(pe, i):
            pe.wait_ge(s_hn, TT * (i + 1))
            for b in range(KD // 2):
                for kk in range(2):
                    for t in range(TT):
                        k = 2 * b + kk
                        col = (kk * TT + t) * P
                        last = nc.tensor.transpose(tp_bank[b][:, col:col + P], hn[:, t, k::KD], ident)
                last.then_inc(s_tp, 1)

        def transpose_act(act, i, out, g, before=0):
            split = i in SPLIT_NORMS
            for b in range(4) if split else (0, 2):
                act.wait_ge(s_tp, 4 * i + b + 1)
                if before:
                    act.wait_ge(s_xT_dve, batches_done(i, b, False))
                for k in (2 * b, 2 * b + 1):
                    src = tp_bank[b][:, (k % 2) * S:(k % 2 + 1) * S]
                    last = nc.scalar.mul((out[0] if split else out)[:, k, :], src, gains[:, g, k:k + 1])
                last.then_inc(s_xT_act, 1)

        def transpose_dve(dve, i, out, g, before=0):
            split = i in SPLIT_NORMS
            for b in range(4) if split else (1, 3):
                dve.wait_ge(s_tp, 4 * i + b + 1)
                if split:
                    dve.wait_ge(s_xT_act, batches_done(i, b, True) + before)
                for k in (2 * b, 2 * b + 1):
                    src = tp_bank[b][:, (k % 2) * S:(k % 2 + 1) * S]
                    if split:
                        last = nc.vector.scalar_tensor_tensor(
                            out=out[1][:, k, :], in0=src, scalar=gains[:, g, k:k + 1],
                            in1=out[0][:, k, :].bitcast(F32), op0=ALU.mult, op1=ALU.subtract)
                    else:
                        last = nc.vector.tensor_scalar(out[:, k, :], src, gains[:, g, k:k + 1], None, ALU.mult)
                last.then_inc(s_xT_dve, 1)

        def xT_ready(engine, i):
            if i not in SPLIT_NORMS:
                engine.wait_ge(s_xT_act, batches_done(i, 2, True))
            engine.wait_ge(s_xT_dve, batches_done(i, 3, False))

        H_DONE = {1: 4, 2: 4 + 4 * EXPERT_GROUPS, 3: 8 + 4 * EXPERT_GROUPS, 4: 8 + 8 * EXPERT_GROUPS}
        ATTN_H0 = H_DONE[2]
        MOE_H0 = [H_DONE[1], H_DONE[3]]

        r_q = area(0, RET_H, 2, S)
        r_k = area(2048, RET_H, 2, S)
        r_v = area(4096, TT, RET_H * RET_DV)
        r_y = area(8192, TT, RET_H * RET_DV)
        r_cos = work[:, 16384:16384 + S]
        r_sin = work[:, 16640:16640 + S]
        r_dec = area(16896, RET_H, DECAY_W)
        r_a = hn[:, 0, 0:2 * DECAY_W].rearrange("p (b n) -> p b n", b=2)
        r_sg = hn[:, 1, :].rearrange("p (b n) -> p b n", b=2)
        r_ta = hn[:, 0, 0:2 * S].rearrange("p (a s) -> p a s", a=2)
        r_tb = hn[:, 0, 2 * S:4 * S].rearrange("p (a s) -> p a s", a=2)
        r_sq = rt[:, 0:RET_DV]
        r_tab = sem("retention_tables_loaded")
        r_qk_done = sem("ret_qk_projected")
        r_rope = sem("ret_qk_rotated")
        r_vg_done = sem("ret_vg_projected")
        r_v_act = sem("ret_v_kept_by_act")
        r_v_dve = sem("ret_v_kept_by_dve")
        r_s_done = sem("ret_scores")
        r_a_ready = sem("ret_scores_decayed")
        r_o_done = sem("ret_heads_out")
        r_o_kept = sem("ret_heads_out_kept")
        r_sumsq = sem("ret_head_squares")
        r_var = sem("ret_head_variance")
        r_std = sem("ret_head_std")
        r_sg_ready = sem("ret_silu_ready")
        r_y_ready = sem("ret_y_ready")
        r_yt_done = sem("ret_y_transposed")
        r_yt_act = sem("ret_yT_by_act")
        r_yt_dve = sem("ret_yT_by_dve")
        r_out_done = sem("ret_out_projected")

        def backwards(view):
            size = view.shape[2]
            return bass.AP(view.tensor, view.offset + size - 1, [view.ap[0], view.ap[1], [-1, size]])

        def retention_pe(pe):
            xT_ready(pe, 0)
            for n in range(4):
                w = halves(n, KD)
                for hh in range(2):
                    i = 2 * n + hh
                    if i >= 4:
                        pe.wait_ge(r_rope, i - 3)
                    for half in range(2):
                        for k in range(KD):
                            c = (2 * hh + half) * P
                            if hh == 0 and half == 0 and k % 4 == 0:
                                half_ready(pe, n, k // 4)
                            last = three_passes(bank[2 + i % 4][:, half * S:(half + 1) * S],
                                                [v[:, k, c:c + P] for v in w],
                                                (x_hi[:, k, :], x_lo[:, k, :]), k == 0, k == KD - 1)
                    if hh == 0:
                        last.then_inc(r_qk_done, 1)
                last.then_inc(s_used, 1)
            bias_pe(pe)
            project_natural(pe, range(4, 7), 0, r_vg_done, r_v_act, r_v_dve)
            for hd in range(RET_H):
                if hd == 2:
                    project_natural(pe, (7,), 3, r_vg_done, r_v_act, r_v_dve)
                    retention_pv(pe, 0)
                if hd >= 2:
                    pe.wait_ge(r_a_ready, hd - 1)
                sc = bank[hd % 2]
                for half in range(2):
                    nc.tensor.matmul(sc[:, 0:S], r_k[:, hd, half, 0:P], r_q[:, hd, half, :],
                                     start=(half == 0), stop=(half == 1))
                for half in range(2):
                    last = nc.tensor.matmul(sc[:, S:S + P], r_k[:, hd, half, P:S], r_q[:, hd, half, P:S],
                                            start=(half == 0), stop=(half == 1))
                last.then_inc(r_s_done, 1)
                if hd >= 2:
                    retention_pv(pe, hd - 1)
            retention_pv(pe, RET_H - 1)
            pe.wait_ge(r_o_kept, 2 * RET_H)
            for n in range(8, 12):
                for t in range(TT):
                    i = 2 * (n - 8) + t
                    if i >= 4:
                        pe.wait_ge(r_sg_ready, i - 3)
                    last = project(pe, bank[2 + i % 4], (x_hi, x_lo), n, t)
                    if t == 0:
                        last.then_inc(r_vg_done, 1)
                last.then_inc(s_used, 1)
            for b in range(RET_KO // 2):
                if b == 0:
                    pe.wait_ge(r_y_ready, 2 * RET_H)
                if b >= 4:
                    pe.wait_ge(r_yt_dve, b - 3)
                for kk in range(2):
                    for t in range(TT):
                        col = (kk * TT + t) * P
                        last = nc.tensor.transpose(tp_bank[b % 4][:, col:col + P], r_y[:, t, 2 * b + kk::RET_KO],
                                                   ident)
                last.then_inc(r_yt_done, 1)
            project_out(pe, FIRST_WOUT, N_WOUT, 4, (yT_hi, yT_lo), r_out_done,
                        {k: (r_yt_dve, k // 2 + 1) for k in range(0, RET_KO, 2)})

        def project(pe, out, x, n, t):
            w = halves(n, KD)
            rows = slice(t * P, (t + 1) * P)
            for k in range(KD):
                if t == 0 and k % 4 == 0:
                    half_ready(pe, n, k // 4)
                last = three_passes(out, [v[:, k, rows] for v in x], [v[:, k, :] for v in w],
                                    k == 0, k == KD - 1)
            return last

        def project_natural(pe, tiles, first, done, by_act, by_dve):
            for i, n in enumerate(tiles, first):
                for t in range(TT):
                    if i >= 2:
                        pe.wait_ge((by_act, by_dve)[t], i - 1)
                    elif i == 0 and t == 0:
                        pe.wait_ge(r_rope, 8)
                    last = project(pe, bank[2 + 2 * (i % 2) + t], (x_hi, x_lo), n, t)
                    if t == 0:
                        last.then_inc(done, 1)
                last.then_inc(s_used, 1)

        def retention_pv(pe, hd):
            pe.wait_ge(r_a_ready, hd + 1)
            if hd == 0:
                pe.wait_ge(r_v_act, 4)
                pe.wait_ge(r_v_dve, 4)
            if hd >= 2:
                pe.wait_ge(r_o_kept, 2 * (hd - 1))
            a = r_a[:, hd % 2, :]
            cols = slice(hd * RET_DV, (hd + 1) * RET_DV)
            o = [bank[2 + 2 * (hd % 2) + t] for t in range(TT)]
            nc.tensor.matmul(o[0], a[:, 0:P], r_v[:, 0, cols], start=True, stop=True).then_inc(r_o_done, 1)
            nc.tensor.matmul(o[1], a[:, P:S], r_v[:, 0, cols], start=True, stop=False)
            nc.tensor.matmul(o[1], a[:, S:S + P], r_v[:, 1, cols], start=False, stop=True).then_inc(r_o_done, 1)

        def project_out(pe, first, tiles, rows, lhs, done, ready):
            kt = tiles * rows
            for j in range(tiles):
                w = halves(first + j, rows)
                for r in range(rows):
                    k = j * rows + r
                    if k in ready:
                        pe.wait_ge(*ready[k])
                    if r % (rows // 2) == 0:
                        half_ready(pe, first + j, r // (rows // 2))
                    for t in range(TT):
                        for nh in range(2):
                            last = three_passes(bank[2 + 2 * t + nh],
                                                [v[:, k, t * P:(t + 1) * P] for v in lhs],
                                                [v[:, r, nh * 512:(nh + 1) * 512] for v in w],
                                                k == 0, k == kt - 1)
                            if k == kt - 1 and (t, nh) != (1, 1):
                                last.then_inc(done, 1)
                last.then_inc(s_used, 1)

        def add_out_dve(dve, first, tiles, done):
            for t in range(TT):
                for nh in range(2):
                    i = 2 * t + nh
                    if i < 3:
                        dve.wait_ge(done, i + 1)
                    else:
                        dve.wait_ge(s_used, first + tiles)
                    hs = h[:, t, nh * 512:(nh + 1) * 512]
                    nc.vector.tensor_tensor(hs, hs, bank[2 + i], ALU.add).then_inc(s_h, 1)

        def retention_act(act):
            for n in range(-2, 4):
                split_next(split_act, act, n, DENSE_A - 1)
            for i in range(4):
                act.wait_ge(r_vg_done, i + 1)
                nc.scalar.copy(r_v[:, 0, i * 512:(i + 1) * 512], bank[2 + 2 * (i % 2)]).then_inc(r_v_act, 1)
                split_next(split_act, act, 4 + i, DENSE_A - 1)
            for i in range(2 * RET_H):
                act.wait_ge(r_o_kept, i + 1)
                if i >= 1:
                    act.wait_ge(r_sumsq, i)
                hd, t = i // 2, i % 2
                nc.scalar.activation(r_sq, r_y[:, t, hd * RET_DV:(hd + 1) * RET_DV], ACT.Square,
                                     accum_out=stat[:, 0, i:i + 1]).then_inc(r_sumsq, 1)
            act.wait_ge(r_var, 1)
            nc.scalar.activation(stat[:, 2, :], stat[:, 1, :], ACT.Sqrt).then_inc(r_std, 1)
            for i in range(2 * RET_H):
                hd, t = i // 2, i % 2
                if t == 0:
                    act.wait_ge(r_vg_done, 4 + hd + 1)
                else:
                    act.wait_ge(s_used, 8 + hd + 1)
                if i >= 2:
                    act.wait_ge(r_y_ready, i - 1)
                nc.scalar.activation(r_sg[:, i % 2, :], bank[2 + i % 4], ACT.Silu).then_inc(r_sg_ready, 1)
                if t == 1 and hd < RET_H - 1:
                    split_next(split_act, act, 8 + hd, DENSE_A - 1)
            act.wait_ge(b_stored, 16)
            for b in range(RET_KO // 2):
                act.wait_ge(r_yt_done, b + 1)
                nc.scalar.copy(yT_hi[:, 2 * b:2 * b + 2, :],
                               tp_bank[b % 4].rearrange("p (k s) -> p k s", k=2)).then_inc(r_yt_act, 1)
            for n in range(FIRST_WOUT - 1, FIRST_WOUT + N_WOUT):
                split_next(split_act, act, n, DENSE_A - 1)

        def retention_dve(dve, chain):
            for n in range(-2, 0):
                split_next(split_dve, dve, n, DENSE_A - 1)
            dve.wait_ge(r_tab, 16 * 3)
            for i in range(8):
                if i % 2 == 0:
                    dve.wait_ge(r_qk_done, i // 2 + 1)
                else:
                    dve.wait_ge(s_used, i // 2 + 1)
                src = bank[2 + i % 4].rearrange("p (a s) -> p a s", a=2)
                dst = (r_q if i < 4 else r_k)[:, i % 4, :, :]
                cos = r_cos.unsqueeze(1).to_broadcast([P, 2, S])
                sin = r_sin.unsqueeze(1).to_broadcast([P, 2, S])
                nc.vector.tensor_tensor(r_ta, src, cos, ALU.mult)
                chain(nc.vector.tensor_tensor(r_tb, src, sin, ALU.mult))
                nc.vector.tensor_tensor(dst[:, 0, :], r_ta[:, 0, :], r_tb[:, 1, :], ALU.subtract)
                nc.vector.tensor_tensor(dst[:, 1, :], r_tb[:, 0, :], r_ta[:, 1, :], ALU.add).then_inc(r_rope, 1)
                dve.wait_ge(r_rope, i + 1)
                if i % 2 == 1:
                    split_next(split_dve, dve, i // 2, DENSE_A - 1)
            bias_dve(dve)
            def decayed(hd):
                dve.wait_ge(r_s_done, hd + 1)
                if hd >= 2:
                    dve.wait_ge(r_o_done, 2 * (hd - 1))
                nc.vector.tensor_tensor(r_a[:, hd % 2, :], bank[hd % 2][:, 0:DECAY_W], r_dec[:, hd, :],
                                        ALU.mult).then_inc(r_a_ready, 1)

            for i in range(4):
                if i == 3:
                    decayed(0)
                    decayed(1)
                dve.wait_ge(s_used, 4 + i + 1)
                nc.vector.tensor_copy(r_v[:, 1, i * 512:(i + 1) * 512],
                                      bank[3 + 2 * (i % 2)]).then_inc(r_v_dve, 1)
                split_next(split_dve, dve, 4 + i, DENSE_A - 1)
            for hd in range(1, RET_H):
                if hd >= 2:
                    decayed(hd)
                keep_heads(dve, hd - 1)
            keep_heads(dve, RET_H - 1)
            dve.wait_ge(r_sumsq, 2 * RET_H)
            nc.vector.tensor_scalar(stat[:, 1, :], stat[:, 0, :], 1.0 / RET_DV, EPS,
                                    ALU.mult, ALU.add).then_inc(r_var, 1)
            dve.wait_ge(r_std, 1)
            chain(nc.vector.reciprocal(stat[:, 1, :], stat[:, 2, :]))
            for i in range(2 * RET_H):
                hd, t = i // 2, i % 2
                dve.wait_ge(r_sg_ready, i + 1)
                y = r_y[:, t, hd * RET_DV:(hd + 1) * RET_DV]
                nc.vector.scalar_tensor_tensor(out=y, in0=y, scalar=stat[:, 1, i:i + 1], in1=r_sg[:, i % 2, :],
                                               op0=ALU.mult, op1=ALU.mult).then_inc(r_y_ready, 1)
                if t == 1 and hd < RET_H - 1:
                    split_next(split_dve, dve, 8 + hd, DENSE_A - 1)
            for b in range(RET_KO // 2):
                dve.wait_ge(r_yt_act, b + 1)
                nc.vector.tensor_tensor(yT_lo[:, 2 * b:2 * b + 2, :],
                                        tp_bank[b % 4].rearrange("p (k s) -> p k s", k=2),
                                        yT_hi[:, 2 * b:2 * b + 2, :].bitcast(F32),
                                        ALU.subtract).then_inc(r_yt_dve, 1)
            for n in range(FIRST_WOUT - 1, FIRST_WOUT + N_WOUT):
                split_next(split_dve, dve, n, DENSE_A - 1)
            add_out_dve(dve, FIRST_WOUT, N_WOUT, r_out_done)

        def keep_heads(dve, hd):
            for t in range(TT):
                dve.wait_ge(r_o_done, 2 * hd + t + 1)
                nc.vector.tensor_copy(r_y[:, t, hd * RET_DV:(hd + 1) * RET_DV],
                                      bank[2 + 2 * (hd % 2) + t]).then_inc(r_o_kept, 1)

        m_sel = area(0, TT, P)
        m_gsel = area(256, TT, P)
        m_gselT = work[:, 512:768]
        m_x = area(1024, KD, P)
        m_sg = work[:, 2048:2560]
        m_hid = work[:, 2560:3072]
        m_hidT = work[:, 3072:3584]
        m_y = work[:, 16384:17408]
        m_t = area(17408, 2, P)
        m = []
        for layer in range(2):
            names = ("logits", "exp_in", "exp_out", "top_in", "top_out", "chosen", "ranked", "slots_ready",
                     "route_w", "step")
            main = ("sel_ready", "gathered", "x_ready", "gselT_done", "gselT_ready", "silu_ready", "hid_ready",
                    "hidT_done", "hidT_ready", "y_done", "y_ready", "combined", "dve")
            over = main + ("used", "h_added", "loaded0", "loaded1", "loaded2")
            m.append({
                **{n: sem(f"moe{layer}_{n}") for n in names},
                "main": {n: sem(f"moe{layer}_group_{n}") for n in main},
                "over": {n: sem(f"moe{layer}_overflow_{n}") for n in over},
            })

        def last_user(j):
            earlier = [i for i in range(-MOE_TILES, j) if MOE_SLOT[i % MOE_TILES] == MOE_SLOT[j]]
            return earlier[-1]

        def free_work_slots(sp, layer, at):
            if layer == 0:
                sp.wait_ge(s_used, FIRST_WOUT + 1)
            else:
                sp.wait_ge(a_sc, 2 * DIL_H)

        def moe_sp(sp, layer):
            first = FIRST_MOE[layer]
            rows = {"gate": exp_gate[layer].rearrange("e (p k) f -> p e (k f)", k=KD),
                    "up": exp_up[layer].rearrange("e (p k) f -> p e (k f)", k=KD),
                    "down": exp_down[layer].rearrange("e (p k) n -> p e (k n)", k=FF // P)}
            tiles = MOE_TILES * EXPERT_GROUPS

            def load(j, expert):
                kind = ("gate", "up", "down")[j // 4]
                sp.dma_start(moe_slot(j).rearrange("p (e c) -> p e c", e=PER_GROUP),
                             rows[kind][:, bass.ds(expert, PER_GROUP),
                                        (j % 4) * 1024:(j % 4 + 1) * 1024]).then_inc(s_ring[MOE_SLOT[j]], 16)

            for j in range(MOE_TILES):
                at = MOE_SLOT[j]
                if at in MOE_SLOT[:j]:
                    sp.wait_ge(s_used, first + last_user(j) + 1)
                elif at in (6, 7):
                    free_work_slots(sp, layer, at)
                elif at < DENSE_RING:
                    sp.wait_ge(s_used, first - DENSE_RING + at + 1)
                else:
                    sp.wait_ge(s_used, first)
                load(j, 0)
            with sp.Fori(1, EXPERT_GROUPS) as it:
                for j in range(MOE_TILES):
                    sp.wait_ge(s_used, it * MOE_TILES + (first + last_user(j) + 1))
                    load(j, it * PER_GROUP)
            sp.wait_ge(m[layer]["slots_ready"], 1)
            count = overflow_blocks(sp, layer)
            o = m[layer]["over"]
            with sp.If(count > 0):
                sp.wait_ge(s_used, first + tiles)
                with sp.Fori(0, count) as b:
                    e = sp.value_load(blocks[0:1, bass.ds(b, 1)], min_val=0, max_val=NE - 1)
                    for j, kind in enumerate(("gate", "up", "down")):
                        sp.wait_ge(o["used"], 3 * b + 1)
                        sp.dma_start(ring[:, j, :].rearrange("p (e c) -> p e c", e=1),
                                     rows[kind][:, bass.ds(e, 1), :]).then_inc(o[f"loaded{j}"], 16)
            return count

        def route_pe(pe, layer):
            s = m[layer]
            i = 1 + 2 * layer
            pe.wait_ge(s["route_w"], 16 * 4)
            for b in range(KD // 2):
                pe.wait_ge(s_xT_act if b % 2 == 0 else s_xT_dve, batches_done(i, b, False))
                for k in (2 * b, 2 * b + 1):
                    for t in range(TT):
                        last = nc.tensor.matmul(bank[2 + t][:, 0:36], xT[:, k, t * P:(t + 1) * P],
                                                w_route[:, k, :], start=(k == 0), stop=(k == KD - 1))
            last.then_inc(s["logits"], 1)
            pe.wait_ge(s["chosen"], 1)
            A = rt[:, 0:64].rearrange("p (t e) -> p t e", t=TT)
            nc.tensor.matmul(bank[4][:, 0:32], tri, A[:, 0, :], start=True, stop=True)
            nc.tensor.matmul(bank[4][:, 32:64], ones, A[:, 0, :], start=True, stop=False)
            nc.tensor.matmul(bank[4][:, 32:64], tri, A[:, 1, :], start=False, stop=True).then_inc(s["ranked"], 1)
            nc.tensor.matmul(bank[5][:, 0:32], ones, A[:, 0, :], start=True,
                             stop=False).then_inc(s["over"]["used"], 1)
            nc.tensor.matmul(bank[5][:, 0:32], ones, A[:, 1, :], start=False, stop=True).then_inc(s["ranked"], 1)

        def route_act(act, layer):
            s = m[layer]
            act.wait_ge(s["exp_in"], 1)
            nc.scalar.activation(m_t[:, 0, 0:8], m_t[:, 0, 0:8], ACT.Exp).then_inc(s["exp_out"], 1)
            act.wait_ge(s["top_in"], 1)
            nc.scalar.activation(m_t[:, 1, 0:2], m_t[:, 1, 0:2], ACT.Exp).then_inc(s["top_out"], 1)

        def route_dve(dve, layer, first_sel):
            s = m[layer]
            chain = Chain(dve, s["step"])
            V = nc.vector
            A = rt[:, 0:64].rearrange("p (t e) -> p t e", t=TT)
            at = [0]
            scratch = xT2[:, :, :].rearrange("p k s -> p (k s)")

            def tmp(*shape):
                size = int(np.prod(shape))
                v = scratch[:, at[0]:at[0] + size]
                at[0] += size
                return v.rearrange("p (a b) -> p a b", b=shape[1]) if len(shape) == 2 else v

            def over_last(v, n):
                return v.unsqueeze(2).to_broadcast([P, TT, n])

            def over_tiles(v, n):
                return v.unsqueeze(1).to_broadcast([P, TT, n])

            own = tmp(NE)
            chain(V.tensor_scalar(own, iota[:, 0:NE], float(SLOTS), None, ALU.mult))
            L = tmp(TT, 36)
            dve.wait_ge(s["logits"], 1)
            dve.wait_ge(s["route_w"], 16 * 4)
            chain(V.tensor_tensor(L, triple[:, 0:1024].rearrange("p (t c) -> p t c", t=TT)[:, :, 0:36],
                                  over_tiles(b_route[:], 36), ALU.add))

            def first_max(scores, n):
                top, low = tmp(TT), tmp(TT)
                place, hot = tmp(TT, n), tmp(TT, n)
                chain(V.tensor_reduce(top, scores, AX, ALU.max))
                chain(V.tensor_tensor(place, scores, over_last(top, n), ALU.is_ge))
                chain(V.scalar_tensor_tensor(out=place, in0=place, scalar=-99.0, in1=over_tiles(iota[:, 0:n], n),
                                             op0=ALU.mult, op1=ALU.add))
                chain(V.tensor_reduce(low, place, AX, ALU.min))
                chain(V.tensor_tensor(hot, place, over_last(low, n), ALU.is_equal))
                return top, hot

            gtop, ghot = first_max(L[:, :, 0:MG], MG)
            V.tensor_tensor(m_t[:, 0, 0:8].rearrange("p (t g) -> p t g", t=TT), L[:, :, 0:MG],
                            over_last(gtop, MG), ALU.subtract).then_inc(s["exp_in"], 1)
            pen = tmp(TT, MG)
            chain(V.tensor_scalar(pen, ghot, FAR, -FAR, ALU.mult, ALU.add))
            E1 = tmp(TT, NE)
            for t in range(TT):
                last = V.tensor_tensor(E1[:, t, :].rearrange("p (g e) -> p g e", g=MG),
                                       L[:, t, MG:].rearrange("p (g e) -> p g e", g=MG),
                                       pen[:, t, :].unsqueeze(2).to_broadcast([P, MG, EPG]), ALU.add)
                chain(last)
            top1, hot1 = first_max(E1, NE)
            E2 = tmp(TT, NE)
            chain(V.scalar_tensor_tensor(out=E2, in0=hot1, scalar=-2.0 * FAR, in1=E1, op0=ALU.mult, op1=ALU.add))
            top2, hot2 = first_max(E2, NE)
            V.tensor_tensor(A, hot1, hot2, ALU.add).then_inc(s["chosen"], 1)
            V.tensor_tensor(m_t[:, 1, 0:2], top2, top1, ALU.subtract).then_inc(s["top_in"], 1)
            psum, r = tmp(TT), tmp(TT)
            dve.wait_ge(s["exp_out"], 1)
            chain(V.tensor_reduce(psum, m_t[:, 0, 0:8].rearrange("p (t g) -> p t g", t=TT), AX, ALU.add))
            dve.wait_ge(s["top_out"], 1)
            chain(V.tensor_scalar(r, m_t[:, 1, 0:2], 1.0, None, ALU.add))
            chain(V.tensor_tensor(r, r, psum, ALU.mult))
            chain(V.reciprocal(gate_of[:, 0, :], r))
            chain(V.tensor_tensor(gate_of[:, 1, :], gate_of[:, 0, :], m_t[:, 1, 0:2], ALU.mult))
            far, slots = tmp(TT, NE), tmp(TT, NE)
            mine = [tmp(TT, NE), tmp(TT, NE)]

            def choose_slots():
                for i, hot in enumerate((hot1, hot2)):
                    last = V.tensor_tensor(mine[i], hot, slots, ALU.mult)
                chain(last)
                for i in range(2):
                    last = V.tensor_reduce(slot_of[:, i, :], mine[i], AX, ALU.add)
                chain(last)

            ranks = bank[4][:, 0:64].rearrange("p (t e) -> p t e", t=TT)
            dve.wait_ge(s["ranked"], 1)
            V.tensor_scalar(far, ranks, float(SLOTS), float(2 * NE * SLOTS), ALU.is_ge, ALU.mult)
            chain(V.tensor_tensor(slots, ranks, over_tiles(own, NE), ALU.add))
            chain(V.tensor_tensor(slots, slots, far, ALU.add))
            choose_slots()
            first_sel()
            more = tmp(NE)
            dve.wait_ge(s["ranked"], 2)
            counts = bank[5][:, 0:32]
            chain(V.tensor_scalar(more, counts, float(SLOTS), None, ALU.is_gt))
            for r_ in range(2, S // SLOTS):
                chain(V.scalar_tensor_tensor(out=more, in0=counts, scalar=float(SLOTS * r_), in1=more,
                                             op0=ALU.is_gt, op1=ALU.add))
            ends, step = more, 1
            while step < NE:
                new = tmp(NE)
                V.tensor_copy(new[:, 0:step], ends[:, 0:step])
                chain(V.tensor_tensor(new[:, step:NE], ends[:, step:NE], ends[:, 0:NE - step], ALU.add))
                ends, step = new, 2 * step
            shift = tmp(NE)
            chain(V.tensor_tensor(shift, ends, more, ALU.subtract))
            chain(V.scalar_tensor_tensor(out=shift, in0=shift, scalar=float(SLOTS), in1=own,
                                         op0=ALU.mult, op1=ALU.subtract))
            chain(V.tensor_scalar(shift, shift, float(NE * SLOTS - SLOTS), None, ALU.add))
            chain(V.scalar_tensor_tensor(out=slots, in0=ranks, scalar=float(SLOTS), in1=over_tiles(shift, NE),
                                         op0=ALU.is_ge, op1=ALU.mult))
            chain(V.tensor_tensor(slots, slots, ranks, ALU.add))
            chain(V.tensor_tensor(slots, slots, over_tiles(own, NE), ALU.add))
            choose_slots()
            whose, expert = tmp(MAX_OVERFLOW, NE), tmp(MAX_OVERFLOW)
            chain(V.tensor_tensor(whose[0:1], ends[0:1].unsqueeze(1).to_broadcast([1, MAX_OVERFLOW, NE]),
                                  iota[0:1, 0:MAX_OVERFLOW].unsqueeze(2).to_broadcast([1, MAX_OVERFLOW, NE]),
                                  ALU.is_le))
            chain(V.tensor_reduce(expert[0:1], whose[0:1], AX, ALU.add))
            chain(V.tensor_scalar(expert[0:1], expert[0:1], float(NE - 1), None, ALU.min))
            V.tensor_copy(blocks[0:1, MAX_OVERFLOW:MAX_OVERFLOW + 1],
                          ends[0:1, NE - 1:NE]).then_inc(s["over"]["h_added"], 1)
            dve.wait_ge(s["over"]["h_added"], 1)
            V.tensor_copy(blocks[0:1, 0:MAX_OVERFLOW], expert[0:1]).then_inc(s["slots_ready"], 1)
            dve.wait_ge(s["slots_ready"], 1)

        def group_pe(pe, layer, it, experts, s, over):
            first = FIRST_MOE[layer]
            M = experts * SLOTS
            pe.wait_ge(s["sel_ready"], 2 * it + 1)
            if over:
                pe.wait_ge(s["h_added"], 4 * it + 1)
                pe.wait_ge(s_h, MOE_H0[layer] + 4 * EXPERT_GROUPS)
            else:
                pe.wait_ge(s_h, MOE_H0[layer] + 4 * it)
            for b in range(2):
                for kk in range(4):
                    for t in range(TT):
                        last = nc.tensor.matmul(bank[b][:, kk * M:(kk + 1) * M], hn[:, t, 4 * b + kk::KD],
                                                m_sel[:, t, 0:M], start=(t == 0), stop=(t == TT - 1))
                last.then_inc(s["gathered"], 1)
            pe.wait_ge(s["sel_ready"], 2 * it + 2)
            for t in range(TT):
                last = nc.tensor.transpose(bank[6][0:M, t * P:(t + 1) * P], m_gsel[:, t, 0:M], ident)
            last.then_inc(s["gselT_done"], 1)
            def used(last, j):
                if not over:
                    last.then_inc(s_used, 1)
                elif j % 4 == 3:
                    last.then_inc(s["used"], 1)

            def weights(j):
                if not over:
                    at = MOE_SLOT[j]
                    loads = loads_before(layer, at) + MOE_SLOT[:j].count(at) + 1
                    pe.wait_ge(s_ring[at], it * (16 * MOE_SLOT.count(at)) + 16 * loads)
                    return moe_slot(j).rearrange("p (e c) -> p e c", e=experts)
                if j % 4 == 0:
                    pe.wait_ge(s[f"loaded{j // 4}"], 16 * it + 16)
                return ring[:, j // 4, (j % 4) * 1024:(j % 4 + 1) * 1024].unsqueeze(1)

            for kind in range(2):
                for c in range(4):
                    if kind == 0 and c % 2 == 0:
                        pe.wait_ge(s["x_ready"], 2 * it + c // 2 + 1)
                    w = weights(4 * kind + c)
                    for kk in range(2):
                        k = 2 * c + kk
                        for e in range(experts):
                            rows = slice(e * SLOTS, (e + 1) * SLOTS)
                            last = nc.tensor.matmul(bank[2 + kind][rows, :], m_x[:, k, rows],
                                                    w[:, e, kk * FF:(kk + 1) * FF],
                                                    start=(k == 0), stop=(k == KD - 1))
                    used(last, 4 * kind + c)
            pe.wait_ge(s["hid_ready"], it + 1)
            for k in range(4):
                last = nc.tensor.transpose(bank[7][:, k * P:(k + 1) * P], m_hid[:, k::4], ident)
            last.then_inc(s["hidT_done"], 1)
            pe.wait_ge(s["hidT_ready"], it + 1)
            for k in range(4):
                w = weights(8 + k)
                for nh in range(2):
                    for e in range(experts):
                        rows = slice(e * SLOTS, (e + 1) * SLOTS)
                        last = nc.tensor.matmul(bank[4 + nh][rows, :],
                                                m_hidT[:, k * P + e * SLOTS:k * P + (e + 1) * SLOTS],
                                                w[:, e, nh * 512:(nh + 1) * 512], start=(k == 0), stop=(k == 3))
                    if k == 3 and nh == 0:
                        last.then_inc(s["y_done"], 1)
                used(last, 8 + k)
            pe.wait_ge(s["gselT_ready"], it + 1)
            for nh in range(2):
                pe.wait_ge(s["y_ready"], 2 * it + nh + 1)
                for t in range(TT):
                    i = 2 * nh + t
                    if i >= 2:
                        if over:
                            pe.wait_ge(s["h_added"], 4 * it + i)
                        else:
                            pe.wait_ge(s_h, MOE_H0[layer] + 4 * it + i - 1)
                    nc.tensor.matmul(bank[t], m_gselT[0:M, t * P:(t + 1) * P], m_y[0:M, nh * 512:(nh + 1) * 512],
                                     start=True, stop=True).then_inc(s["combined"], 1)

        def group_act(act, layer, it, experts, s, over):
            first = FIRST_MOE[layer]
            M = experts * SLOTS

            def tiles_done(j):
                if over:
                    act.wait_ge(s["used"], 3 * it + j // 4 + 1)
                else:
                    act.wait_ge(s_used, it * MOE_TILES + first + j)

            for b in range(2):
                act.wait_ge(s["gathered"], 2 * it + b + 1)
                for kk in range(4):
                    k = 4 * b + kk
                    last = nc.scalar.mul(m_x[:, k, 0:M], bank[b][:, kk * M:(kk + 1) * M],
                                         gains[:, 1 + 2 * layer, k:k + 1])
                last.then_inc(s["x_ready"], 1)
            act.wait_ge(s["gselT_done"], it + 1)
            if over:
                act.wait_ge(s["h_added"], 4 * it + 1)
            else:
                act.wait_ge(s_h, MOE_H0[layer] + 4 * it)
            nc.scalar.copy(m_gselT[0:M, :], bank[6][0:M, 0:S]).then_inc(s["gselT_ready"], 1)
            tiles_done(4)
            nc.scalar.activation(m_sg[0:M, :], bank[2][0:M, :], ACT.Silu).then_inc(s["silu_ready"], 1)
            act.wait_ge(s["hidT_done"], it + 1)
            nc.scalar.copy(m_hidT[:, :], bank[7]).then_inc(s["hidT_ready"], 1)
            act.wait_ge(s["y_done"], it + 1)
            nc.scalar.copy(m_y[0:M, 0:512], bank[4][0:M, :]).then_inc(s["y_ready"], 1)
            tiles_done(12)
            nc.scalar.copy(m_y[0:M, 512:1024], bank[5][0:M, :]).then_inc(s["y_ready"], 1)

        def next_slots(dve, chain, M):
            nc.vector.tensor_scalar(slot_of[:, 0, :], slot_of[:, 0, :], -float(M), None, ALU.add)
            chain(nc.vector.tensor_scalar(slot_of[:, 1, :], slot_of[:, 1, :], -float(M), None, ALU.add))

        def select(dve, n, M, s):
            V = nc.vector
            chain = Chain(dve, s["dve"], n * DVE_PER_GROUP)
            for t in range(TT):
                V.tensor_scalar(m_t[:, t, 0:M], iota[:, 0:M], slot_of[:, 1, t:t + 1], None, ALU.is_equal)
                last = V.tensor_scalar(m_gsel[:, t, 0:M], iota[:, 0:M], slot_of[:, 0, t:t + 1], None, ALU.is_equal)
            chain(last)
            for t in range(TT):
                last = V.tensor_tensor(m_sel[:, t, 0:M], m_t[:, t, 0:M], m_gsel[:, t, 0:M], ALU.add)
            last.then_inc(s["sel_ready"], 1)
            for t in range(TT):
                last = V.tensor_scalar(m_gsel[:, t, 0:M], m_gsel[:, t, 0:M], gate_of[:, 0, t:t + 1], None,
                                       ALU.mult)
            chain(last)
            for t in range(TT):
                last = V.scalar_tensor_tensor(out=m_gsel[:, t, 0:M], in0=m_t[:, t, 0:M],
                                              scalar=gate_of[:, 1, t:t + 1], in1=m_gsel[:, t, 0:M],
                                              op0=ALU.mult, op1=ALU.add)
            last.then_inc(s["sel_ready"], 1)

        def group_dve(dve, layer, it, experts, s, over):
            first = FIRST_MOE[layer]
            M = experts * SLOTS
            V = nc.vector
            chain = Chain(dve, s["dve"], it * DVE_PER_GROUP + 2)
            if over:
                select(dve, it, M, s)
            dve.wait_ge(s["silu_ready"], it + 1)
            if over:
                dve.wait_ge(s["used"], 3 * it + 3)
            else:
                dve.wait_ge(s_used, it * MOE_TILES + first + 8)
            V.tensor_tensor(m_hid[0:M, :], m_sg[0:M, :], bank[3][0:M, :], ALU.mult).then_inc(s["hid_ready"], 1)
            if not over:
                next_slots(dve, chain, M)
                dve.wait_ge(s["gselT_done"], it + 1)
                select(dve, it + 1, M, s)
            for i in range(4):
                nh, t = i // 2, i % 2
                dve.wait_ge(s["combined"], 4 * it + i + 1)
                hs = h[:, t, nh * 512:(nh + 1) * 512]
                V.tensor_tensor(hs, hs, bank[t], ALU.add).then_inc(s["h_added"] if over else s_h, 1)
            if over:
                next_slots(dve, chain, M)

        def moe_engine(engine, layer, group):
            with engine.Fori(0, EXPERT_GROUPS) as it:
                group(engine, layer, it, PER_GROUP, m[layer]["main"], False)
            engine.wait_ge(m[layer]["slots_ready"], 1)
            count = overflow_blocks(engine, layer)
            with engine.If(count > 0):
                with engine.Fori(0, count) as b:
                    group(engine, layer, b, 1, m[layer]["over"], True)

        def overflow_blocks(engine, layer):
            return engine.value_load(blocks[0:1, MAX_OVERFLOW:MAX_OVERFLOW + 1], min_val=0,
                                     max_val=MAX_OVERFLOW)

        PAIRS = GROUPS * DIL_H // 2
        DEPTH_DEN = 4
        d_q = area(0, PAIRS, S)
        d_k = area(PAIRS * S, PAIRS, S)
        d_v = area(2 * PAIRS * S, TT, QCOLS)
        flat_x = xT[:, :, :].rearrange("p k s -> p (k s)")
        flat_x2 = xT2[:, :, :].rearrange("p k s -> p (k s)")
        flat_hn = hn[:, :, :].rearrange("p t d -> p (t d)")
        d_raw = [flat_hn[:, i * 512:(i + 1) * 512] for i in range(2)]
        d_nrm = [flat_hn[:, 1024 + i * 512:1024 + (i + 1) * 512] for i in range(2)]
        d_sq = rt[:, 0:512]
        d_ss = sb("head_squares", [P, 2, 8])
        d_sd = sb("head_std", [P, 2, 8])
        d_bias = [flat_x[:, i * GROUPS * S:(i + 1) * GROUPS * S].rearrange("p (g n) -> p g n", g=GROUPS)
                  for i in range(2)]
        W0, W1 = GROUPS * P, GROUPS * S
        d_spare = sb("pT_piece", [P, W0])
        scores = place("scores", (DENSE_RING + 1) * TILE, [P, TILE])
        d_p = [scores[:, i * (W0 + W1):(i + 1) * (W0 + W1)] for i in range(3)]
        pieces = [f[:, i * W0:(i + 1) * W0] for f in (flat_x2, flat_hn) for i in range(5)]
        pieces += [d_spare[:], flat_x[:, 2 * W1:2 * W1 + W0]]
        d_pT = [pieces[3 * i:3 * i + 3] for i in range(4)]
        d_max = sb("row_max", [P, 2, TT])
        d_neg = sb("row_max_negated", [P, 2, TT])
        d_den = sb("row_sum", [P, DEPTH_DEN, TT])
        d_inv = sb("row_sum_inverse", [P, DEPTH_DEN, TT])
        bias_tab = work[:, 12288:12288 + BW]
        bias_mask = work[:, 12288 + BW:12288 + 2 * BW]
        bias_rel = work[:, 12288 + 2 * BW:12288 + 2 * BW + GROUPS * DIL_H]
        bias_out = work[:, 13500:13500 + BW]

        s_btab = sem("bias_tables_loaded")
        b_done = sem("bias_rows_made")
        b_kept = sem("bias_rows_kept")
        b_stored = sem("bias_rows_stored")
        b_loaded = [sem(f"bias_loaded{i}") for i in range(2)]
        s_qkg = sem("qk_gain_loaded")
        q_done = sem("dil_tile_projected")
        q_raw = sem("dil_raw_kept")
        q_sq = sem("dil_squared")
        q_var = sem("dil_variance")
        q_std = sem("dil_std")
        q_nrm = sem("dil_normed")
        q_tp = sem("dil_transposed")
        q_kept = sem("dil_qk_kept")
        v_act = sem("dil_v_by_act")
        v_dve = sem("dil_v_by_dve")
        a_sc = sem("att_scores")
        a_sum = sem("att_biased")
        a_neg = sem("att_max_ready")
        a_exp = sem("att_exp")
        a_tp = sem("att_transposed")
        a_pT_act = sem("att_pT_by_act")
        a_pT_dve = sem("att_pT_by_dve")
        a_o = sem("att_out")
        a_kept = sem("att_out_kept")
        a_nrm = sem("att_normed")
        a_side = sem("att_shared_bank_written")
        a_aT_act = sem("att_aT_by_act")
        a_aT_dve = sem("att_aT_by_dve")
        a_proj = sem("att_projected")

        def bias_pe(pe):
            pe.wait_ge(s_btab, 16 * 3)
            nc.tensor.matmul(bank[7][0:GROUPS * DIL_H, 0:BW], bias_rel[0:BUCKETS, :], bias_tab[0:BUCKETS, :],
                             start=True, stop=True).then_inc(b_done, 1)

        def bias_dve(dve):
            dve.wait_ge(b_done, 1)
            nc.vector.tensor_tensor(bias_out[0:GROUPS * DIL_H, :], bank[7][0:GROUPS * DIL_H, 0:BW],
                                    bias_mask[0:GROUPS * DIL_H, :], ALU.add).then_inc(b_kept, 1)

        UNITS = 2 * 2 * N_KV
        LAST_B = FIRST_QKV + DENSE_B - 1

        def dilated_pe(pe):
            xT_ready(pe, 2)

            def turn(u):
                if u == 0:
                    pe.wait_ge(s_xT_dve, batches_done(3, -2, False))
                pe.wait_ge(q_nrm, u + 1)
                if u >= 2:
                    pe.wait_ge(q_kept, u - 1)
                for b in range(4):
                    last = nc.tensor.transpose(bank[u % 2][:, b * P:(b + 1) * P],
                                               d_nrm[u % 2][:, b * P:(b + 1) * P], ident)
                last.then_inc(q_tp, 1)

            for i in range(2 * N_KV):
                src = (xq_hi, xq_lo) if i < N_KV else (x_hi, x_lo)
                for t in range(TT):
                    u = 2 * i + t
                    if u >= 4:
                        pe.wait_ge(q_raw, u - 3)
                    last = project(pe, bank[2 + u % 4], src, FIRST_QKV + i, t)
                    if t == 0:
                        last.then_inc(q_done, 1)
                    else:
                        last.then_inc(s_used, 1)
                    if u >= 1:
                        turn(u - 1)
            for i in range(N_KV):
                n = FIRST_QKV + 2 * N_KV + i
                for t in range(TT):
                    if i >= 2:
                        pe.wait_ge((v_act, v_dve)[t], i - 1)
                    elif i == 0 and t == 0:
                        pe.wait_ge(q_raw, UNITS)
                    last = project(pe, bank[2 + 2 * (i % 2) + t], (x_hi, x_lo), n, t)
                    if t == 0:
                        last.then_inc(q_done, 1)
                last.then_inc(s_used, 1)
                if i == 0:
                    turn(UNITS - 1)
            pe.wait_ge(q_kept, UNITS)
            pe.wait_ge(v_act, N_KV)
            pe.wait_ge(v_dve, N_KV)
            def values(pr, columns):
                o = bank[7][:, 0:S]
                for c in columns:
                    t, g, kt = (0, c, 0) if c < GROUPS else (1, (c - GROUPS) // 2, (c - GROUPS) % 2)
                    for odd in range(2):
                        hd = 2 * pr + odd
                        cols = slice(g * D + hd * DIL_DH, g * D + (hd + 1) * DIL_DH)
                        last = nc.tensor.matmul(o[odd * DIL_DH:(odd + 1) * DIL_DH, t * P:(t + 1) * P],
                                                d_v[:, kt, cols],
                                                d_pT[hd % 4][c // 3][:, (c % 3) * P:(c % 3 + 1) * P],
                                                start=(g == 0 and kt == 0), stop=(g == GROUPS - 1 and kt == t))
                    if c == 3 * GROUPS - 1:
                        last.then_inc(a_o, 1)

            for i in range(DIL_H // 2 + 2):
                if i < DIL_H // 2:
                    if i >= 1:
                        pe.wait_ge(a_sum, 4 * i)
                    for t in range(TT):
                        n = (t + 1) * P
                        for g in range(GROUPS):
                            pr = g * DIL_H // 2 + i
                            for odd in range(2):
                                if t == 1 and g == GROUPS - 1 and odd == 0:
                                    pe.wait_ge(a_side, i + 1)
                                rows = slice(odd * DIL_DH, (odd + 1) * DIL_DH)
                                sc = bank[odd] if t == 0 else triple[:, odd * W1:(odd + 1) * W1]
                                last = nc.tensor.matmul(sc[:, g * n:(g + 1) * n],
                                                        d_q[rows, pr, t * P:(t + 1) * P],
                                                        d_k[rows, pr, 0:n], start=True, stop=True)
                                if g == GROUPS - 1:
                                    last.then_inc(a_sc, 1)
                                elif t == 1 and g == 0 and odd == 1:
                                    last.then_inc(a_side, 1)
                if i >= 2:
                    pe.wait_ge(a_pT_act, 4 * (i - 2) + 4)
                    pe.wait_ge(a_pT_dve, 2 * (i - 2) + 2)
                for step in range(6):
                    hd, b = 2 * (i - 1) + step // 3, step % 3
                    if 1 <= i <= DIL_H // 2:
                        if b == 0:
                            pe.wait_ge(a_nrm, hd + 1)
                        if b == 0 and hd >= 1:
                            pe.wait_ge(a_pT_dve, hd)
                        elif b == 1 and hd >= 1:
                            pe.wait_ge(a_pT_act, 2 * hd)
                        elif b == 2:
                            pe.wait_ge(a_pT_act, 2 * hd + 1)
                        for j in range(3):
                            c = (3 * b + j) * P
                            last = nc.tensor.transpose(bank[5 + (3 * hd + b) % 2][:, j * P:(j + 1) * P],
                                                       d_p[hd % 3][:, c:c + P], ident)
                        last.then_inc(a_tp, 1)
                    if i >= 2 and step >= 1:
                        if step == 1 and i >= 3:
                            pe.wait_ge(a_kept, i - 2)
                        values(i - 2, range(2 * step - 2, min(2 * step, 3 * GROUPS)))
            project_out(pe, FIRST_WO, N_WO, 4, (aT_hi, aT_lo), a_proj, {0: (a_aT_dve, 2), 4: (a_aT_dve, 4)})

        def dilated_act(act):
            act.wait_ge(s_qkg, 16 * 4)

            def keep(u):
                act.wait_ge(q_tp, u + 1)
                i, t = u // 2, u % 2
                j = i % N_KV
                src = bank[u % 2].rearrange("p (a s) -> p a s", a=4)
                nc.scalar.mul((d_q if i < N_KV else d_k)[:, 4 * j:4 * j + 4, t * P:(t + 1) * P],
                              backwards(src) if i < N_KV else src,
                              qk_gain[:, 1 - i // N_KV, j // 2:j // 2 + 1]).then_inc(q_kept, 1)

            split_act(act, FIRST_QKV + 1)
            for u in range(UNITS):
                i, t = u // 2, u % 2
                if t == 0:
                    act.wait_ge(q_done, i + 1)
                else:
                    act.wait_ge(s_used, FIRST_QKV + i + 1)
                if u >= 2:
                    act.wait_ge(q_nrm, u - 1)
                nc.scalar.copy(d_raw[u % 2], bank[2 + u % 4]).then_inc(q_raw, 1)
                act.wait_ge(q_raw, u + 1)
                nc.scalar.activation(d_sq, d_raw[u % 2], ACT.Square).then_inc(q_sq, 1)
                if u >= 1:
                    keep(u - 1)
                act.wait_ge(q_var, u + 1)
                nc.scalar.activation(d_sd[:, u % 2, :], d_ss[:, u % 2, :], ACT.Sqrt).then_inc(q_std, 1)
                if t == 1:
                    split_next(split_act, act, FIRST_QKV + i, LAST_B)
            for i in range(N_KV):
                act.wait_ge(q_done, 2 * N_KV + i + 1)
                nc.scalar.copy(d_v[:, 0, i * 512:(i + 1) * 512], bank[2 + 2 * (i % 2)]).then_inc(v_act, 1)
                if i == 0:
                    keep(UNITS - 1)
                split_next(split_act, act, FIRST_QKV + 2 * N_KV + i, FIRST_WO)
            def keep_heads_out(pr):
                act.wait_ge(a_o, pr + 1)
                nc.scalar.copy(d_v[:, :, pr * P:(pr + 1) * P],
                               bank[7][:, 0:S].rearrange("p (t s) -> p t s", t=TT)
                               ).then_inc(a_kept, 1)

            for j in range(DIL_H // 2 + 1):
                if j >= 3:
                    keep_heads_out(j - 3)
                for hd in (2 * j - 2, 2 * j - 1) if j >= 1 else ():
                    if hd >= 4 and hd % 2 == 0:
                        act.wait_ge(a_o, j - 2)
                    for b in (0, 2):
                        act.wait_ge(a_tp, 3 * hd + b + 1)
                        nc.scalar.copy(d_pT[hd % 4][b], bank[5 + (3 * hd + b) % 2][:, 0:W0]).then_inc(a_pT_act, 1)
                for i in (2 * j, 2 * j + 1) if j < DIL_H // 2 else ():
                    act.wait_ge(a_neg, i + 1)
                    for t in range(TT):
                        p = d_p[i % 3][:, 0:W0] if t == 0 else d_p[i % 3][:, W0:W0 + W1]
                        nc.scalar.activation(p, p, ACT.Exp, bias=d_neg[:, i % 2, t:t + 1],
                                             accum_out=d_den[:, i % DEPTH_DEN, t:t + 1]).then_inc(a_exp, 1)
            keep_heads_out(DIL_H // 2 - 2)
            keep_heads_out(DIL_H // 2 - 1)
            act.wait_ge(a_kept, DIL_H // 2)
            for b in range(KD // 2):
                ks, t = slice(4 * (b // 2), 4 * (b // 2) + 4), b % 2
                nc.scalar.copy(aT_hi[:, ks, t * P:(t + 1) * P], heads_out(ks, t)).then_inc(a_aT_act, 1)
            split_act(act, FIRST_WO + 1)

        def heads_out(ks, t):
            return backwards(d_v[:, t, ks.start * P:ks.stop * P].rearrange("p (k s) -> p k s", s=P))

        def dilated_dve(dve, chain):
            split_dve(dve, FIRST_QKV + 1)
            for u in range(UNITS):
                dve.wait_ge(q_sq, u + 1)
                ss = d_ss[:, u % 2, :]
                chain(nc.vector.tensor_reduce(ss, d_sq.rearrange("p (h d) -> p h d", d=DIL_DH), AX, ALU.add))
                nc.vector.tensor_scalar(ss, ss, 1.0 / DIL_DH, EPS, ALU.mult, ALU.add).then_inc(q_var, 1)
                dve.wait_ge(q_std, u + 1)
                sd = d_sd[:, u % 2, :]
                chain(nc.vector.reciprocal(sd, sd))
                if u >= 2:
                    dve.wait_ge(q_tp, u - 1)
                scale = DIL_DH ** -0.5 if u < UNITS // 2 else 1.0
                nc.vector.scalar_tensor_tensor(
                    out=d_nrm[u % 2].rearrange("p (h d) -> p h d", d=DIL_DH),
                    in0=d_raw[u % 2].rearrange("p (h d) -> p h d", d=DIL_DH), scalar=scale,
                    in1=sd.unsqueeze(2).to_broadcast([P, 8, DIL_DH]),
                    op0=ALU.mult, op1=ALU.mult).then_inc(q_nrm, 1)
                if u % 2 == 1:
                    split_next(split_dve, dve, FIRST_QKV + u // 2, LAST_B)
            for i in range(N_KV):
                dve.wait_ge(s_used, FIRST_QKV + 2 * N_KV + i + 1)
                nc.vector.tensor_copy(d_v[:, 1, i * 512:(i + 1) * 512],
                                      bank[3 + 2 * (i % 2)]).then_inc(v_dve, 1)
                split_next(split_dve, dve, FIRST_QKV + 2 * N_KV + i, FIRST_WO)
            def biased(i, t):
                if t == 0:
                    dve.wait_ge(b_loaded[i % 2], 16 * (i // 2 + 1))
                    if i >= 3:
                        dve.wait_ge(a_tp, 3 * (i - 2))
                    src, add = bank[i % 2][:, 0:W0], d_bias[i % 2][:, :, P:S]
                    dst = d_p[i % 3][:, 0:W0]
                else:
                    src, add = triple[:, (i % 2) * W1:(i % 2 + 1) * W1], d_bias[i % 2]
                    dst = d_p[i % 3][:, W0:W0 + W1]
                dve.wait_ge(a_sc, 4 * (i // 2) + 2 * t + i % 2 + 1)
                three = "p (g n) -> p g n"
                nc.vector.tensor_tensor_reduce(
                    out=dst.rearrange(three, g=GROUPS), in0=src.rearrange(three, g=GROUPS), in1=add,
                    scale=1.0, scalar=-3.0e38, op0=ALU.add, op1=ALU.max,
                    accum_out=d_max[:, i % 2, t:t + 1]).then_inc(a_sum, 1)
                if t == 0:
                    return
                dve.wait_ge(a_sum, 2 * i + 2)
                nc.vector.tensor_scalar(d_neg[:, i % 2, :], d_max[:, i % 2, :], -1.0, None,
                                        ALU.mult).then_inc(a_neg, 1)

            def divided(hd):
                dve.wait_ge(a_exp, 2 * hd + 2)
                inverse = d_inv[:, hd % DEPTH_DEN, :]
                chain(nc.vector.reciprocal(inverse, d_den[:, hd % DEPTH_DEN, :]))
                for t in range(TT):
                    p = d_p[hd % 3][:, 0:W0] if t == 0 else d_p[hd % 3][:, W0:W0 + W1]
                    last = nc.vector.tensor_scalar(p, p, inverse[:, t:t + 1], None, ALU.mult)
                last.then_inc(a_nrm, 1)

            def turned(hd):
                if hd >= 4:
                    dve.wait_ge(a_o, hd // 2 - 1)
                dve.wait_ge(a_tp, 3 * hd + 2)
                nc.vector.tensor_copy(d_pT[hd % 4][1], bank[5 + (3 * hd + 1) % 2][:, 0:W0]).then_inc(a_pT_dve, 1)

            for j in range(DIL_H // 2 + 1):
                for odd in range(2):
                    if j < DIL_H // 2:
                        biased(2 * j + odd, 0)
                        if odd == 1:
                            biased(2 * j + 1, 1)
                    if j >= 1:
                        turned(2 * j - 2 + odd)
                    if j < DIL_H // 2 and odd == 0:
                        biased(2 * j, 1)
                for odd in range(2) if j < DIL_H // 2 else ():
                    divided(2 * j + odd)
            for b in range(KD // 2):
                dve.wait_ge(a_aT_act, b + 1)
                ks, t = slice(4 * (b // 2), 4 * (b // 2) + 4), b % 2
                rows = slice(t * P, (t + 1) * P)
                nc.vector.tensor_tensor(aT_lo[:, ks, rows], heads_out(ks, t), aT_hi[:, ks, rows].bitcast(F32),
                                        ALU.subtract).then_inc(a_aT_dve, 1)
            split_dve(dve, FIRST_WO + 1)
            add_out_dve(dve, FIRST_WO, N_WO, a_proj)

        block = ctx.enter_context(nc.Block())

        @block.sync
        def _(sp):
            sp.dma_start(h[:, :, :], x[0].rearrange("(t p) d -> p t d", p=P)).then_inc(s_x, 16)
            sp.dma_start(kept[:, :], constants[:, 0:C_KEPT]).then_inc(s_small, 16)
            sp.dma_start(gains[:, 0:4:2, :], mixer_norm.rearrange("l (p k) -> p l k", k=KD)).then_inc(s_small, 16)
            sp.dma_start(gains[:, 1:4:2, :], ffn_norm.rearrange("l (p k) -> p l k", k=KD)).then_inc(s_small, 16)
            sp.dma_start(gains[:, 4, :], kv_norm.rearrange("(p k) -> p k", k=KD)).then_inc(s_small, 16)
            for i in range(N_WIN):
                load_tile(sp, FIRST_WIN + i, win[:, :, i * COLS:(i + 1) * COLS], KD)
            for i in range(N_WOUT):
                load_tile(sp, FIRST_WOUT + i, wout[:, 4 * i:4 * i + 4, :], 4)
            overflow = moe_sp(sp, 0)
            sp.wait_ge(m[0]["over"]["used"], 3 * overflow + 1)
            for i in range(3 * N_KV):
                if i < N_KV:
                    src = wq[:, :, i * COLS:(i + 1) * COLS]
                else:
                    src = wkv[:, :, (i - N_KV) * COLS:(i - N_KV + 1) * COLS]
                load_tile(sp, FIRST_QKV + i, src, KD)
            for i in range(N_WO):
                load_tile(sp, FIRST_WO + i, wo[:, 4 * i:4 * i + 4, :], 4)
            overflow = moe_sp(sp, 1)
            sp.wait_ge(m[1]["over"]["h_added"], 4 * overflow + 1)
            for i in range(4):
                nh, t = i // 2, i % 2
                cols = slice(nh * 512, (nh + 1) * 512)
                sp.wait_ge(s_h, H_DONE[4] - 3 + i)
                sp.dma_start(out[0, t * P:(t + 1) * P, cols], h[:, t, cols]).then_inc(s_out, 16)
            sp.wait_ge(s_out, 16 * 4)

        @block.gpsimd
        def _(pool):
            def route_loads(layer):
                s = m[layer]["route_w"]
                pool.dma_start(w_route[:, :, 0:MG], router_grp[layer].rearrange("(p k) g -> p k g", k=KD)
                               ).then_inc(s, 16)
                pool.dma_start(w_route[:, :, MG:], router_exp[layer].rearrange("(p k) e -> p k e", k=KD)
                               ).then_inc(s, 16)
                pool.dma_start(b_route[:, 0:MG], router_grp_b[layer:layer + 1, :].to_broadcast([P, MG])
                               ).then_inc(s, 16)
                pool.dma_start(b_route[:, MG:], router_exp_b[layer:layer + 1, :].to_broadcast([P, NE])
                               ).then_inc(s, 16)

            pool.dma_start(r_cos, constants[:, C_COS:C_COS + S]).then_inc(r_tab, 16)
            pool.dma_start(r_sin, constants[:, C_SIN:C_SIN + S]).then_inc(r_tab, 16)
            pool.dma_start(work[:, 16896:16896 + RET_H * DECAY_W],
                           constants[:, C_DECAY:C_DECAY + RET_H * DECAY_W]).then_inc(r_tab, 16)
            pool.dma_start(bias_tab, constants[:, C_BUCKET:C_BUCKET + BW]).then_inc(s_btab, 16)
            pool.dma_start(bias_mask, constants[:, C_MASK:C_MASK + BW]).then_inc(s_btab, 16)
            pool.dma_start(bias_rel[0:BUCKETS, :], rel_bias).then_inc(s_btab, 16)
            for half in range(2):
                rows = slice(half * DIL_DH, (half + 1) * DIL_DH)
                pool.dma_start(qk_gain[rows, 0, :], k_norm.rearrange("g d -> d g"),
                               allow_slow_non_contiguous=True).then_inc(s_qkg, 16)
                pool.dma_start(qk_gain[rows, 1, :], q_norm[0].rearrange("g d -> d g"),
                               allow_slow_non_contiguous=True).then_inc(s_qkg, 16)
            route_loads(0)
            pool.wait_ge(b_kept, 1)
            pool.dma_start(bias_rows, bias_out[0:GROUPS * DIL_H, :]).then_inc(b_stored, 16)
            pool.wait_ge(m[0]["slots_ready"], 1)
            route_loads(1)
            pool.wait_ge(b_stored, 16)
            pool.wait_ge(q_done, 3 * N_KV)
            pool.wait_ge(s_used, FIRST_WO)
            for hd in range(DIL_H):
                if hd >= 2:
                    pool.wait_ge(a_sum, 2 * (hd - 1))
                src = bass.AP(bias_rows.tensor, hd * BW, [[1, P], [DIL_H * BW, GROUPS], [1, S]])
                pool.dma_start(d_bias[hd % 2], src).then_inc(b_loaded[hd % 2], 16)

        @block.scalar
        def _(act):
            norm_act(act, 0)
            act.wait_ge(s_small, 64)
            transpose_act(act, 0, (x_hi, x_lo), 0)
            retention_act(act)
            norm_act(act, 1)
            transpose_act(act, 1, xT, 1)
            route_act(act, 0)
            moe_engine(act, 0, group_act)
            split_act(act, FIRST_QKV, (0,))
            norm_act(act, 2)
            transpose_act(act, 2, (xq_hi, xq_lo), 2)
            split_act(act, FIRST_QKV, (1,))
            transpose_act(act, 2, (x_hi, x_lo), 4, 4)
            dilated_act(act)
            norm_act(act, 3)
            transpose_act(act, 3, xT, 3)
            route_act(act, 1)
            moe_engine(act, 1, group_act)

        @block.vector
        def _(dve):
            chain = Chain(dve, s_dv)
            norm_dve(dve, chain, 0)
            dve.wait_ge(s_small, 64)
            transpose_dve(dve, 0, (x_hi, x_lo), 0)
            retention_dve(dve, chain)
            norm_dve(dve, chain, 1)
            transpose_dve(dve, 1, xT, 1)
            route_dve(dve, 0, lambda: select(dve, 0, PER_GROUP * SLOTS, m[0]["main"]))
            moe_engine(dve, 0, group_dve)
            norm_dve(dve, chain, 2)
            split_dve(dve, FIRST_QKV, (0,))
            transpose_dve(dve, 2, (xq_hi, xq_lo), 2)
            split_dve(dve, FIRST_QKV, (1,))
            transpose_dve(dve, 2, (x_hi, x_lo), 4, 4)
            dilated_dve(dve, chain)
            norm_dve(dve, chain, 3)
            transpose_dve(dve, 3, xT, 3)
            route_dve(dve, 1, lambda: select(dve, 0, PER_GROUP * SLOTS, m[1]["main"]))
            moe_engine(dve, 1, group_dve)

        @block.tensor
        def _(pe):
            pe.wait_ge(s_small, 64)
            transpose_pe(pe, 0)
            retention_pe(pe)
            transpose_pe(pe, 1)
            route_pe(pe, 0)
            moe_engine(pe, 0, group_pe)
            transpose_pe(pe, 2)
            dilated_pe(pe)
            transpose_pe(pe, 3)
            route_pe(pe, 1)
            moe_engine(pe, 1, group_pe)


_INS = ["x", "ret_w_in", "ret_w_out", "kv_norm", "w_kv", "k_norm", "dil_wq", "q_norm", "dil_wo", "rel_bias",
        "mixer_norm", "ffn_norm", "router_grp", "router_grp_b", "router_exp", "router_exp_b",
        "exp_gate", "exp_up", "exp_down"]


def kernel(**inputs):
    import numpy as _np
    import concourse.bacc as _bacc
    from concourse.bass_utils import run_bass_kernel_spmd as _run

    nc = _bacc.Bacc("TRN2", target_bir_lowering=False, num_devices=1)
    arrays, args = {}, []
    for name in _INS:
        arrays[f"in_{name}"] = _np.ascontiguousarray(inputs[name])
    arrays["shape_constants"] = shape_constants()
    for name, a in arrays.items():
        args.append(nc.dram_tensor(name, a.shape, mybir.dt.from_np(a.dtype), kind="ExternalInput").ap())
    args.append(nc.dram_tensor("out_0", (1, S, D), F32, kind="ExternalOutput").ap())
    build(nc, *args)
    r = _run(nc, [arrays], core_ids=[0])
    return r.results[0]["out_0"]
```
